# Optimizing a Trainium2 kernel written in Bass

```python
import math
import jax, jax.numpy as jnp
from jax import lax
import numpy as np

D_MODEL = 2048
BATCH = 1
SEQ = 256
DEPTH = 1

CHUNK = 64
PLE_DIM = 256
ATT_HEAD_DIM = 64
ATT_HEADS = D_MODEL // ATT_HEAD_DIM
ATT_KV_HEADS = ATT_HEADS // 8
WINDOW = 128
WIN_CHUNKS = WINDOW // CHUNK
ROPE_THETA = 10000.0
ATT_WIDTH = ATT_HEADS * ATT_HEAD_DIM
ATT_KV_WIDTH = ATT_KV_HEADS * ATT_HEAD_DIM
DN_KEY_DIM = 128
DN_VAL_DIM = 128
DN_HEADS = D_MODEL // DN_VAL_DIM
DN_QK_WIDTH = DN_HEADS * DN_KEY_DIM
DN_V_WIDTH = DN_HEADS * DN_VAL_DIM
DN_CONV_CH = 2 * DN_QK_WIDTH + DN_V_WIDTH
CONV_WIDTH = 4
D_FF = ((8 * D_MODEL + 3 * 256 - 1) // (3 * 256)) * 256
IN_SPLITS = (ATT_WIDTH, ATT_KV_WIDTH, ATT_KV_WIDTH, DN_QK_WIDTH, DN_QK_WIDTH, DN_V_WIDTH,
             DN_V_WIDTH, DN_HEADS, DN_HEADS, D_MODEL, D_MODEL)
IN_IS_VALUE = (False, False, True, False, False, True, False, False, False, False, False)
IN_WIDTH = sum(IN_SPLITS)
LN_EPS = 1e-5
RMS_EPS = 1e-6
L2_EPS = 1e-6
DEEPNORM_ALPHA = (2.0 * DEPTH) ** 0.25
DEEPNORM_BETA = (8.0 * DEPTH) ** -0.25

kernel_name = 'hybrid_swa_sink_gated_deltanet_deepnorm_block'

def split_cols(t, sizes):
    idx = [int(s) for s in np.cumsum(sizes)[:-1]]
    return jnp.split(t, idx, axis=-1)

def layer_norm(x, g, b):
    xf = x.astype(jnp.float32)
    mu = jnp.mean(xf, axis=-1, keepdims=True)
    var = jnp.mean(jnp.square(xf - mu), axis=-1, keepdims=True)
    y = (xf - mu) * lax.rsqrt(var + LN_EPS) * g.astype(jnp.float32) + b.astype(jnp.float32)
    return y.astype(x.dtype)

def rope(t, pos):
    half = t.shape[-1] // 2
    inv_freq = ROPE_THETA ** (-jnp.arange(half, dtype=jnp.float32) / half)
    ang = pos.astype(jnp.float32)[:, None] * inv_freq[None, :]
    cos = jnp.cos(ang)[None, :, None, :]
    sin = jnp.sin(ang)[None, :, None, :]
    tf = t.astype(jnp.float32)
    t1, t2 = tf[..., :half], tf[..., half:]
    return jnp.concatenate([t1 * cos - t2 * sin, t2 * cos + t1 * sin], axis=-1).astype(t.dtype)

def sliding_window_sink_attention(q, k, v, sinks):
    B, S = q.shape[:2]
    nc = S // CHUNK
    grp = ATT_HEADS // ATT_KV_HEADS
    qc = q.reshape(B, nc, CHUNK, ATT_KV_HEADS, grp, ATT_HEAD_DIM).astype(jnp.float32)
    kc = k.reshape(B, nc, CHUNK, ATT_KV_HEADS, ATT_HEAD_DIM)
    vc = v.reshape(B, nc, CHUNK, ATT_KV_HEADS, ATT_HEAD_DIM)

    def band(t):
        parts = []
        for w in range(WIN_CHUNKS):
            shift = WIN_CHUNKS - 1 - w
            parts.append(jnp.pad(t, ((0, 0), (shift, 0), (0, 0), (0, 0), (0, 0)))[:, :nc])
        return jnp.concatenate(parts, axis=2)

    kw = band(kc).astype(jnp.float32)
    vw = band(vc)
    slot_src = jnp.arange(nc)[:, None] - (WIN_CHUNKS - 1 - jnp.arange(WIN_CHUNKS * CHUNK) // CHUNK)[None, :]
    valid = slot_src >= 0
    s = jnp.einsum('bnqhgd,bnkhd->bnhgqk', qc, kw) * (ATT_HEAD_DIM ** -0.5)
    s = jnp.where(valid[None, :, None, None, None, :], s, -jnp.inf)
    sink = sinks.astype(jnp.float32).reshape(1, 1, ATT_KV_HEADS, grp, 1, 1)
    m = jnp.maximum(jnp.max(s, axis=-1, keepdims=True), sink)
    e = jnp.exp(s - m)
    prob = e / (jnp.sum(e, axis=-1, keepdims=True) + jnp.exp(sink - m))
    o = jnp.einsum('bnhgqk,bnkhd->bnqhgd', prob.astype(vw.dtype), vw)
    return o.reshape(B, S, ATT_WIDTH)

def causal_depthwise_conv(t, w):
    C = t.shape[-1]
    return lax.conv_general_dilated(t, w[:, None, :].astype(t.dtype), window_strides=(1,),
                                    padding=[(CONV_WIDTH - 1, 0)],
                                    dimension_numbers=('NWC', 'WIO', 'NWC'),
                                    feature_group_count=C)

def l2_normalize(t):
    tf = t.astype(jnp.float32)
    return tf * lax.rsqrt(jnp.sum(tf * tf, axis=-1, keepdims=True) + L2_EPS)

def gated_delta_rule_chunked(q, k, v, g, beta):
    B, S, H, dk = q.shape
    dv = v.shape[-1]
    nc = S // CHUNK
    f32 = jnp.float32

    def to_chunks(t):
        t = t.astype(f32).reshape((B, nc, CHUNK) + t.shape[2:])
        return jnp.moveaxis(t, 3, 2)

    q, k, v, g, beta = map(to_chunks, (q, k, v, g, beta))
    gcum = jnp.cumsum(g, axis=-1)
    ii = jnp.arange(CHUNK)
    causal = ii[:, None] >= ii[None, :]
    strict = ii[:, None] > ii[None, :]
    decay = jnp.exp(jnp.where(causal, gcum[..., :, None] - gcum[..., None, :], -jnp.inf))
    k_beta = k * beta[..., None]
    a_mat = jnp.einsum('bnhid,bnhjd->bnhij', k_beta, k) * decay * strict
    eye = jnp.eye(CHUNK, dtype=f32)
    rhs = jnp.concatenate([v * beta[..., None], k_beta * jnp.exp(gcum)[..., None]], axis=-1)
    sol = lax.linalg.triangular_solve(eye + a_mat, rhs, left_side=True, lower=True,
                                      unit_diagonal=True)
    u, w = sol[..., :dv], sol[..., dv:]
    qk = jnp.einsum('bnhid,bnhjd->bnhij', q, k) * decay
    q_dec = q * jnp.exp(gcum)[..., None]
    k_dec = k * jnp.exp(gcum[..., -1:] - gcum)[..., None]
    chunk_decay = jnp.exp(gcum[..., -1])

    def step(state, inp):
        q_i, k_i, u_i, w_i, qk_i, d_i = inp
        v_new = u_i - jnp.einsum('bhcd,bhde->bhce', w_i, state)
        o_i = jnp.einsum('bhcd,bhde->bhce', q_i, state) + jnp.einsum('bhij,bhje->bhie', qk_i, v_new)
        state = state * d_i[..., None, None] + jnp.einsum('bhcd,bhce->bhde', k_i, v_new)
        return state, o_i

    xs = tuple(jnp.moveaxis(t, 1, 0) for t in (q_dec, k_dec, u, w, qk, chunk_decay))
    state0 = jnp.zeros((B, H, dk, dv), f32)
    _, o = lax.scan(step, state0, xs)
    return jnp.transpose(o, (1, 0, 3, 2, 4)).reshape(B, S, H, dv)

def gated_rms_norm(o, z, gain):
    of = o.astype(jnp.float32)
    n = of * lax.rsqrt(jnp.mean(of * of, axis=-1, keepdims=True) + RMS_EPS) * gain.astype(jnp.float32)
    return n * jax.nn.silu(z.astype(jnp.float32))

def hybrid_mixer(h, pos, w_in, b_in, att_sinks, dn_conv_w, dn_a_log, dn_dt_bias, dn_norm_g,
                 w_br_att, w_br_dn, w_out):
    B, S, _ = h.shape
    proj = h @ w_in + b_in
    aq, ak, av, dq, dk_, dv_, dz, db, da, ga, gb = split_cols(proj, IN_SPLITS)
    aq = rope(aq.reshape(B, S, ATT_HEADS, ATT_HEAD_DIM), pos)
    ak = rope(ak.reshape(B, S, ATT_KV_HEADS, ATT_HEAD_DIM), pos)
    av = av.reshape(B, S, ATT_KV_HEADS, ATT_HEAD_DIM)
    o_att = sliding_window_sink_attention(aq, ak, av, att_sinks)
    qkv = jax.nn.silu(causal_depthwise_conv(jnp.concatenate([dq, dk_, dv_], axis=-1), dn_conv_w))
    cq, ck, cv = split_cols(qkv, (DN_QK_WIDTH, DN_QK_WIDTH, DN_V_WIDTH))
    q = l2_normalize(cq.reshape(B, S, DN_HEADS, DN_KEY_DIM)) * (DN_KEY_DIM ** -0.5)
    k = l2_normalize(ck.reshape(B, S, DN_HEADS, DN_KEY_DIM))
    v = cv.reshape(B, S, DN_HEADS, DN_VAL_DIM)
    beta = jax.nn.sigmoid(db.astype(jnp.float32))
    g = -jnp.exp(dn_a_log.astype(jnp.float32)) * jax.nn.softplus(
        da.astype(jnp.float32) + dn_dt_bias.astype(jnp.float32))
    o_dn = gated_delta_rule_chunked(q, k, v, g, beta)
    o_dn = gated_rms_norm(o_dn, dz.reshape(B, S, DN_HEADS, DN_VAL_DIM), dn_norm_g)
    o_dn = o_dn.reshape(B, S, DN_V_WIDTH).astype(h.dtype)
    y_att = o_att @ w_br_att
    y_dn = o_dn @ w_br_dn
    merged = jax.nn.sigmoid(ga) * y_att + jax.nn.sigmoid(gb) * y_dn
    return merged @ w_out

def swiglu(h, w_gate, w_up, w_down):
    return (jax.nn.silu(h @ w_gate) * (h @ w_up)) @ w_down

def setup_inputs(seed: int = 0) -> dict:
    key = jax.random.key(seed)
    ks = jax.random.split(key, 32)
    f32 = jnp.float32

    def nrm(k, shape, scale):
        return jax.random.normal(k, shape, f32) * scale

    col_scale = jnp.concatenate([jnp.full((n,), DEEPNORM_BETA if is_v else 1.0, f32)
                                 for n, is_v in zip(IN_SPLITS, IN_IS_VALUE)])
    dt = jnp.exp(jax.random.uniform(ks[7], (DEPTH, DN_HEADS), f32, math.log(1e-3), math.log(1e-1)))
    return {
        'x': nrm(ks[0], (BATCH, SEQ, D_MODEL), 1.0),
        'p': nrm(ks[1], (DEPTH, BATCH, SEQ, PLE_DIM), 1.0),
        'w_in': nrm(ks[2], (DEPTH, D_MODEL, IN_WIDTH), D_MODEL ** -0.5) * col_scale,
        'b_in': nrm(ks[3], (DEPTH, IN_WIDTH), 0.02),
        'att_sinks': nrm(ks[4], (DEPTH, ATT_HEADS), 1.0),
        'dn_conv_w': nrm(ks[5], (DEPTH, CONV_WIDTH, DN_CONV_CH), CONV_WIDTH ** -0.5),
        'dn_a_log': jnp.log(jax.random.uniform(ks[6], (DEPTH, DN_HEADS), f32, 1.0, 16.0)),
        'dn_dt_bias': dt + jnp.log(-jnp.expm1(-dt)),
        'dn_norm_g': 1.0 + nrm(ks[8], (DEPTH, DN_VAL_DIM), 0.05),
        'w_br_att': nrm(ks[9], (DEPTH, ATT_WIDTH, D_MODEL), ATT_WIDTH ** -0.5 * DEEPNORM_BETA),
        'w_br_dn': nrm(ks[10], (DEPTH, DN_V_WIDTH, D_MODEL), DN_V_WIDTH ** -0.5 * DEEPNORM_BETA),
        'w_out': nrm(ks[11], (DEPTH, D_MODEL, D_MODEL), D_MODEL ** -0.5 * DEEPNORM_BETA),
        'ln_mix_g': 1.0 + nrm(ks[12], (DEPTH, D_MODEL), 0.05),
        'ln_mix_b': nrm(ks[13], (DEPTH, D_MODEL), 0.02),
        'w_ffn_gate': nrm(ks[14], (DEPTH, D_MODEL, D_FF), D_MODEL ** -0.5 * DEEPNORM_BETA),
        'w_ffn_up': nrm(ks[15], (DEPTH, D_MODEL, D_FF), D_MODEL ** -0.5 * DEEPNORM_BETA),
        'w_ffn_down': nrm(ks[16], (DEPTH, D_FF, D_MODEL), D_FF ** -0.5 * DEEPNORM_BETA),
        'w_ple_gate': nrm(ks[17], (DEPTH, D_MODEL, D_MODEL), D_MODEL ** -0.5),
        'b_ple_gate': nrm(ks[18], (DEPTH, D_MODEL), 0.02),
        'w_ple_proj': nrm(ks[19], (DEPTH, PLE_DIM, D_MODEL), PLE_DIM ** -0.5 * DEEPNORM_BETA),
        'ln_ffn_g': 1.0 + nrm(ks[20], (DEPTH, D_MODEL), 0.05),
        'ln_ffn_b': nrm(ks[21], (DEPTH, D_MODEL), 0.02),
    }

def reference(x, p, w_in, b_in, att_sinks, dn_conv_w, dn_a_log, dn_dt_bias, dn_norm_g,
              w_br_att, w_br_dn, w_out, ln_mix_g, ln_mix_b, w_ffn_gate, w_ffn_up, w_ffn_down,
              w_ple_gate, b_ple_gate, w_ple_proj, ln_ffn_g, ln_ffn_b):
    S = x.shape[1]
    pos = jnp.arange(S, dtype=jnp.int32)
    h = x
    for i in range(DEPTH):
        mix = hybrid_mixer(h, pos, w_in[i], b_in[i], att_sinks[i], dn_conv_w[i], dn_a_log[i],
                           dn_dt_bias[i], dn_norm_g[i], w_br_att[i], w_br_dn[i], w_out[i])
        h = layer_norm(DEEPNORM_ALPHA * h + mix, ln_mix_g[i], ln_mix_b[i])
        ffn = swiglu(h, w_ffn_gate[i], w_ffn_up[i], w_ffn_down[i])
        ple = jax.nn.sigmoid(h @ w_ple_gate[i] + b_ple_gate[i]) * (p[i] @ w_ple_proj[i])
        h = layer_norm(DEEPNORM_ALPHA * h + ffn + ple, ln_ffn_g[i], ln_ffn_b[i])
    return h


_drawn_inputs = setup_inputs


def setup_inputs(seed=0):
    import zlib

    import numpy as np

    out = dict(_drawn_inputs(seed))
    spreads = {}
    factors = {'b_in': 8.0,
     'att_sinks': 8.0,
     'dn_a_log': 3.518,
     'dn_norm_g': 8.0,
     'w_br_att': 3.827,
     'ln_mix_b': 2.85,
     'b_ple_gate': 28.295,
     'ln_ffn_b': 2.772}
    for name, (base, spread) in spreads.items():
        noise = np.random.default_rng([zlib.crc32(name.encode()), seed]).standard_normal(out[name].shape)
        drawn = base * np.exp(spread * noise) if base else spread * noise
        out[name] = __import__('jax').numpy.asarray(drawn.astype(out[name].dtype))
    for name, factor in factors.items():
        out[name] = (out[name] * factor).astype(out[name].dtype)
    return out
```

```python
from contextlib import ExitStack

import numpy as np

import concourse.bass as bass
from concourse import mybir

F32 = mybir.dt.float32
F32R = mybir.dt.float32r
ALU = mybir.AluOpType
ACT = mybir.ActivationFunctionType
AX = mybir.AxisListType
ds = bass.ds

P = 128
T = 256
TT = T // P
D = 2048
KT = D // P
CH = 64
NCH = T // CH
HEADS = 16
PAIRS = HEADS // 2
ATT_HEADS, HD, KV = 32, 64, 4
FF = 5632
FT = FF // P
PLE = 256
ALPHA = 2.0 ** 0.25
LN_EPS, RMS_EPS, L2_EPS = 1e-5, 1e-6, 1e-6
BIG = 1e30
TAIL = (0, 4, 6, 9, 12, 17, 20, 23)
NORMS = 1
LAG = 2
ATT_SCALE = HD ** -0.5
AQ, AK, AV = 0, 2048, 2304
DQ, DK, DV, DZ = 2560, 4608, 6656, 8704
DB, GA, GB = 10752, 10784, 12832

U_QKV = 0
U_LOOP = U_QKV + 5 * 4
U_YA = U_LOOP + PAIRS * 8
U_YD = U_YA + 8 * 4
U_OUT = U_YD + 8 * 4
U_PLE = U_OUT + 4 * 4
U_FFN = U_PLE + 2 * 9
P_AT, GATE_AT = (0, 52), (4, 20, 36, 56)
U_DOWN = U_FFN + (FF // 256) * 4
U_END = U_DOWN + 4 * (FT // 4)
RAW = 4
RING = 8
LEAD = 6

LEVELS = (1, 2, 4, 8, 16, 32)
C_IDENT, C_CUM, C_CAUSAL, C_ONES = 0, 128, 256, 384
C_NEGM = 512
C_NEGMT = C_NEGM + 128 * len(LEVELS)
C_COS = C_NEGMT + 128 * len(LEVELS)
C_SIN = C_COS + TT * 32
C_PREV = C_SIN + TT * 32
C_KEEP = C_PREV + PAIRS
C_SAME, C_SEL0, C_SEL1 = C_KEEP, C_KEEP + 128, C_KEEP + 256
C_END = C_KEEP + 384


ONCE = {
    "scalar_setup": ("wdb_hi", "ealog", "bcol", "p_hi", "eneg", "yabs", "eabs", "eg", "kdecs", "dall"),
    "vector_setup": ("wdb_lo", "dbda_rows", "dt_sum", "taps_in", "p_lo", "halves", "sinks_in", "graw",
                     "gcol_in", "gsums_out", "k_rot", "pad_zero", "nbeg"),
    "tensor_setup": ("dbda", "set_cols", "gsums", "k_cols"),
}
ONCE_OF = {name: (kind, n + 1) for kind, names in ONCE.items() for n, name in enumerate(names)}


def due(name, v=1):
    return ONCE_OF[name][1] if name in ONCE_OF else v


SERIES = {"tanh": (0, 4), "a_level": (1, 5), "inverse": (0, 5), "inverse_t": (0, 6),
          "y_prod": (1, 5), "y_out": (1, 5), "x_prod": (1, 4), "xt_prod": (1, 5), "v_prod": (0, 4), "v_out": (0, 4),
          "o_prod": (0, 4), "rhs": (1, 3), "state": (0, 3), "ks_prod": (1, 3)}


def nth(name, n, p):
    first, count = SERIES[name]
    return count * p + n - first + 1


def constants():
    c = np.zeros((P, C_END), np.float32)
    i = np.arange(P)[:, None]
    j = np.arange(P)[None, :]
    same = (i // CH) == (j // CH)
    c[:, C_IDENT:C_IDENT + P] = i == j
    c[:, C_CUM:C_CUM + P] = same & (i <= j)
    c[:, C_CAUSAL:C_CAUSAL + P] = np.where(same & (j <= i), 0.0, BIG)
    c[:, C_ONES:C_ONES + P] = 1.0
    for n, s in enumerate(LEVELS):
        m = -((i // (2 * s) == j // (2 * s)) & (i // s % 2 == 1) & (j // s % 2 == 0)).astype(np.float32)
        c[:, C_NEGM + P * n:C_NEGM + P * (n + 1)] = m
        c[:, C_NEGMT + P * n:C_NEGMT + P * (n + 1)] = m.T
    c[:, C_SAME:C_SAME + P] = same
    c[:, C_SEL0:C_SEL0 + P] = i < CH
    c[:, C_SEL1:C_SEL1 + P] = i >= CH
    half = HD // 2
    inv = np.float32(10000.0) ** (-np.arange(half, dtype=np.float32) / np.float32(half))
    ang = (np.arange(T, dtype=np.float32)[:, None] * inv[None, :].astype(np.float32)).astype(np.float32)
    for t in range(TT):
        c[:, C_COS + 32 * t:C_COS + 32 * t + 32] = np.cos(ang[t * P:(t + 1) * P].astype(np.float64))
        c[:, C_SIN + 32 * t:C_SIN + 32 * t + 32] = np.sin(ang[t * P:(t + 1) * P].astype(np.float64))
    c[:, C_PREV:C_PREV + PAIRS:2] = -BIG
    return c


class Pos:

    def __init__(self, q, per=0, i=0):
        self.q, self.dyn = q, per * i

    def val(self, n, k=1):
        return (self.q + n) * k + self.dyn * k

    def slot(self, n):
        return (self.q + n) % RING

    def raw(self, n):
        u = (self.q + n) // 4
        return u % RAW, 16 * (u // RAW + 1) + self.dyn


def build(nc, A, out):
    ctx = ExitStack()
    with ctx:
        at = [nc.sbuf_base + (-nc.sbuf_base) % 32]

        def place(name, shape, dtype=F32, where=None):
            size = 4
            for n in shape[1:]:
                size *= n
            size += -size % 32
            off = at[0] if where is None else where[0]
            (at if where is None else where)[0] += size
            assert off + size <= nc.sbuf_usable_end, (name, off, size)
            return nc.alloc_sbuf_tensor_at(name, shape, dtype, offset=off)

        raw = place("raw", [P, RAW, 2048])
        hi = place("hi", [P, RING, 512], F32R)
        lo = place("lo", [P, RING, 512], F32R)
        x_at = at[0]
        xh = place("xh", [P, KT, T], F32R)
        xl = place("xl", [P, KT, T], F32R)
        epsc = place("epsc", [P, 8])
        lnst = place("lnst", [P, TT, 32])
        qb_at = at[0]
        qbuf = place("qbuf", [P, PAIRS, 512])
        odn_at = at[0]
        odn = place("odn", [P, KT, T])
        cst = place("cst", [P, C_KEEP])
        bcol = place("bcol", [P, 97])
        cw = place("cw", [P, 4, 48])
        graw = place("graw", [P, TT, HEADS])
        gcol = place("gcol", [P, TT, HEADS])
        beta = place("beta", [P, TT, HEADS])
        bhalf = place("bhalf", [P, TT, HEADS])
        nbeg = place("nbeg", [P, TT, HEADS])
        kdecs = place("kdecs", [P, TT, HEADS])
        dall = place("dall", [P, NCH, HEADS])
        ghalf = place("ghalf", [P, 1])
        hbias = place("hbias", [P, 32])
        sinks = place("sinks", [P, PAIRS, 8])
        ph = place("ph", [P, 2, T], F32R)
        pl = place("pl", [P, 2, T], F32R)
        kTall = place("kTall", [P, PAIRS, 192])
        vall = place("vall", [P, PAIRS, 2, HD])
        ws_at = at[0]
        cq = place("cq", [P, 2, T])
        ck = place("ck", [P, 2, T])
        cv = place("cv", [P, 2, T])
        zb = place("zb", [P, 2, T])
        pad = place("pad", [P, 2, T + 3])
        kh = place("kh", [P, 2, T])
        qh = place("qh", [P, 2, T])
        qd = place("qd", [P, 2, T])
        egb = place("egb", [P, 4, P])
        Am = place("Am", [P, 4, P])
        AT = place("AT", [P, 4, P])
        Tm = place("Tm", [P, 4, P])
        Um = place("Um", [P, 4, P])
        Ym = place("Ym", [P, 4, P])
        tmp = place("tmp", [P, 4, P])
        tmu = place("tmu", [P, 4, P])
        QK = place("QK", [P, 4, P])
        QKT = place("QKT", [P, 4, P])
        bv = place("bv", [P, 4, P])
        kd = place("kd", [P, 4, P])
        S = place("S", [P, 2, P])
        rr = place("rr", [P, 2, P])
        vn = place("vn", [P, 2, P])
        o = [at[0]]
        pTE = place("pTE", [P, 512], where=o)
        pTO = place("pTO", [P, 512], where=o)
        qr = place("qr", [P, 8, HD])
        qT = place("qT", [P, 2, 4, CH])
        sE = place("sE", [P, 4, P])
        sO = place("sO", [P, 4, P])
        kS = place("kS", [P, 192])
        vS = place("vS", [P, 2, HD])
        sm = place("sm", [P, 8, 8])
        o = [odn_at]
        xrow = place("xrow", [P, TT, D], where=o)
        o = [ws_at]
        rowsA = place("rowsA", [P, 3, P], where=o)
        biasq = place("biasq", [P, 2560], where=o)
        krow = place("krow", [P, TT, 512], where=o)
        krot = place("krot", [P, TT, KV, 2, HD], where=o)
        krt = place("krt", [P, TT, 16, 32], where=o)
        st = place("st", [P, 16, TT, HEADS], where=o)
        wdb = place("wdb", [P, KT, 32], where=o)
        wdbh = place("wdbh", [P, KT, 32], F32R, where=o)
        wdbl = place("wdbl", [P, KT, 32], F32R, where=o)
        cst2 = place("cst2", [P, C_END - C_KEEP], where=o)
        gbias = place("gbias", [P, 64], where=o)
        sinkraw = place("sinkraw", [P, ATT_HEADS], where=o)
        prow = place("prow", [P, TT, PLE], where=o)
        dbda = place("dbda", [P, TT, 32], where=o)
        o = [ws_at]
        bh = place("bh", [P, KT, T], F32R, where=o)
        bl = place("bl", [P, KT, T], F32R, where=o)
        gt = place("gt", [P, 2, 2, T], where=o)
        yt = place("yt", [P, 2, 2, T], where=o)
        o = [qb_at]
        merged = place("merged", [P, KT, T], where=o)
        o = [qb_at]
        res = place("res", [P, TT, D], where=o)
        hid_at = o[0]
        hh = place("hh", [P, FT, T], F32R, where=o)
        hl = place("hl", [P, FT, T], F32R, where=o)
        ff = place("ff", [P, 2, 2, T], where=o)
        o = [ws_at]
        lng = place("lng", [P, D], where=o)
        lnb = place("lnb", [P, D], where=o)
        pb = place("pb", [P, D], where=o)
        pg = place("pg", [P, 2, TT, 512], where=o)
        lns = place("lns", [P, TT, 32], where=o)
        o = [x_at]
        lng2 = place("lng2", [P, D], where=o)
        lnb2 = place("lnb2", [P, D], where=o)

        dense = ctx.enter_context(nc.psum_tensor("dense", [P, 4, 512], F32))
        C = ctx.enter_context(nc.psum_tensor("chain", [P, 4, 512], F32))

        sems = {}

        def sem(name):
            name = ONCE_OF[name][0] if name in ONCE_OF else name
            if name not in sems:
                sems[name] = ctx.enter_context(nc.semaphore(name))
            return sems[name]

        ident = cst[:, C_IDENT:C_IDENT + P]
        ones = cst[:, C_ONES:C_ONES + P]
        negm = [cst[:, C_NEGM + P * n:C_NEGM + P * n + P] for n in range(6)]
        negmt = [cst[:, C_NEGMT + P * n:C_NEGMT + P * n + P] for n in range(6)]

        def four(m):
            return m.unsqueeze(1).to_broadcast([P, 4, P])

        def per_row(m, p):
            return m[:, :, ds(2 * p, 2)].rearrange("p t h -> p h t").unsqueeze(3).to_broadcast([P, 2, TT, P])

        def blocks(m):
            return m.rearrange("p (h t) c -> p h t c", h=2) if len(m.shape) == 3 else \
                m.rearrange("p (h t c) -> p h t c", h=2, t=TT)

        def flat(m):
            return m.rearrange("p a b -> p (a b)")

        def flat2(m):
            return m.rearrange("p a b -> p (a b)")

        def att_cols(b):
            return qbuf[:, 2 * (b // 2):2 * (b // 2) + 2, :].rearrange("p t (u c) -> p u t c", u=4)[
                :, 2 * (b % 2):2 * (b % 2) + 2]

        lnst_of = {1: lns, 2: lnst}
        w_in = A["w_in"][0]
        block = ctx.enter_context(nc.Block())

        def unit_cols(w, h, col, n=1024):
            return w[1024 * h:1024 * h + 1024, col].rearrange("(k p) n -> p k n", p=P)

        @block.sync
        def _(sp):
            def load(pos, u, src, shape=(8, 256)):
                n = 4 * u
                slot, val = pos.raw(n)
                if (pos.q + n) // 4 >= RAW:
                    sp.wait_ge(sem("lo_ready"), pos.val(n - 4 * RAW + 4))
                dst = raw[:, slot, :shape[0] * shape[1]].rearrange("p (k n) -> p k n", k=shape[0])
                sp.dma_start(dst, src).then_inc(sem(f"raw_in{slot}"), 16)

            def rows_unit(w, k0, col):
                return w[P * k0:P * k0 + 512, col].rearrange("(k p) n -> p k n", p=P)

            sp.dma_start(cst[:], A["consts"][:, 0:C_KEEP]).then_inc(sem("cst_in"), 16)
            for t in range(TT):
                sp.dma_start(xrow[:, t, :], A["x"][0][t * P:(t + 1) * P]).then_inc(sem(f"x_in{t}"), 16)
            for j in range(4):
                load(Pos(0), j, rows_unit(w_in, 4 * j, slice(AK, AK + 512)), (4, 512))
            with sp.Fori(0, 2) as m:
                for e in range(2):
                    for j in range(4):
                        load(Pos(16 + 16 * e, 32, m), j,
                             rows_unit(w_in, 4 * j, ds(1024 * m + 512 * e, 512)), (4, 512))
            sp.wait_ge(sem("rows_out"), 1)
            v4 = vall[:].rearrange("p (g t) n d -> p g t n d", g=KV)
            kr = krow[:, :, 256:512].rearrange("p t (g d) -> p t g d", g=KV)
            sp.dma_start(v4[0:64, :, 1, 0, :], kr[64:128, 0, :, :]).then_inc(sem("v_moved"), 16)
            sp.dma_start(v4[64:128, :, 0, 0, :], kr[0:64, 0, :, :]).then_inc(sem("v_moved"), 16)
            sp.dma_start(v4[64:128, :, 1, 0, :], kr[0:64, 1, :, :]).then_inc(sem("v_moved"), 16)
            with sp.Fori(0, PAIRS) as i:
                for s, off in enumerate((DQ, DK, DV, DZ)):
                    for h in range(2):
                        load(Pos(4 * U_LOOP, 32, i), 2 * s + h, unit_cols(w_in, h, ds(off + 256 * i, 256)))
            for off, w, base in ((GA, A["w_br_att"][0], U_YA), (GB, A["w_br_dn"][0], U_YD)):
                with sp.Fori(0, 8) as j:
                    for h in range(2):
                        load(Pos(4 * base, 16, j), h, unit_cols(w_in, h, ds(32 * (8 * j + off // 32), 256)))
                    for h in range(2):
                        load(Pos(4 * base, 16, j), 2 + h, unit_cols(w, h, ds(256 * j, 256)))
            with sp.Fori(0, 4) as c:
                for j in range(4):
                    load(Pos(4 * U_OUT, 16, c), j, rows_unit(A["w_out"][0], 4 * j, ds(512 * c, 512)), (4, 512))
            pos = Pos(4 * U_PLE)
            for g in range(4):
                if g in (0, 3):
                    m = g // 2
                    load(pos, P_AT[m] // 4, A["w_ple_proj"][0][:, 1024 * m:1024 * m + 1024].rearrange(
                        "(k p) n -> p k n", p=P), (2, 1024))
                for j in range(4):
                    load(pos, GATE_AT[g] // 4 + j,
                         rows_unit(A["w_ple_gate"][0], 4 * j, slice(512 * g, 512 * g + 512)), (4, 512))
            with sp.Fori(0, FF // 256) as f:
                for g, w in enumerate((A["w_ffn_gate"][0], A["w_ffn_up"][0])):
                    for h in range(2):
                        load(Pos(4 * U_FFN, 16, f), 2 * g + h, unit_cols(w, h, ds(256 * f, 256)))
            for c in range(4):
                for j in range(FT // 4):
                    load(Pos(4 * U_DOWN), (FT // 4) * c + j,
                         rows_unit(A["w_ffn_down"][0], 4 * j, slice(512 * c, 512 * c + 512)), (4, 512))
            for n in range(2 * TT):
                t, c = n // 2, slice(1024 * (n % 2), 1024 * (n % 2) + 1024)
                sp.wait_ge(sem("out_rows"), n + 1)
                sp.dma_start(out[0][t * P:(t + 1) * P, c], res[:, t, c]).then_inc(sem("stored"), 16)
            sp.wait_ge(sem("stored"), 16 * 2 * TT)

        @block.gpsimd
        def _(pool):
            pool.memset(kTall[:].rearrange("p (g t) n -> p g t n", t=TT)[:, :, 0, 0:64], 0.0).then_inc(sem("k_zero"), 1)
            pool.memset(vall[:].rearrange("p (g t) n d -> p g t n d", t=TT)[0:64, :, 0, 0, :], 0.0).then_inc(sem("v_zero"), 1)
            b_in = A["b_in"][0]
            rows = lambda v: v.rearrange("(r p) -> r p", p=P)
            pool.dma_start(wdb[:], w_in[:, DB:DB + 32].rearrange("(k p) n -> p k n", p=P)).then_inc(sem("wdb_in"), 16)
            pool.dma_start(gbias[:, 0:32], b_in[DB:DB + 32].partition_broadcast(P)).then_inc(sem("g_in"), 16)
            pool.dma_start(gbias[:, 32:48], A["dn_a_log"][0].partition_broadcast(P)).then_inc(sem("g_in"), 16)
            pool.dma_start(gbias[:, 48:64], A["dn_dt_bias"][0].partition_broadcast(P)).then_inc(sem("g_in"), 16)
            pool.dma_start(biasq[:], b_in[0:2560].partition_broadcast(P)).then_inc(sem("bq_in"), 16)
            pool.dma_start(rowsA[0:64, 0, :], rows(b_in[DQ:DB])).then_inc(sem("rows_in"), 16)
            pool.dma_start(rowsA[64:96, 0, :], rows(b_in[GA:GB + D])).then_inc(sem("rows_in"), 16)
            pool.dma_start(rowsA[96:97, 0, :], A["dn_norm_g"][0:1]).then_inc(sem("rows_in"), 16)
            taps = A["dn_conv_w"][0].rearrange("j (t p) -> (j t) p", p=P)
            pool.dma_start(rowsA[:, 1, :], taps[0:128]).then_inc(sem("rows_in"), 16)
            pool.dma_start(rowsA[0:64, 2, :], taps[128:192]).then_inc(sem("rows_in"), 16)
            pool.dma_start(cst2[:], A["consts"][:, C_KEEP:C_END]).then_inc(sem("cst2_in"), 16)
            pool.dma_start(prow[:], A["p"][0, 0].rearrange("(t p) n -> p t n", p=P)).then_inc(sem("p_in"), 16)
            pool.dma_start(sinkraw[:], A["att_sinks"][0].partition_broadcast(P)).then_inc(sem("sink_in"), 16)
            with pool.Fori(0, PAIRS) as p:
                pool.wait_ge(sem("ATc"), p + 1)
                for n in range(1, 6):
                    if n >= 3:
                        pool.wait_ge(sem("y_prod"), nth("y_prod", n - 2, p))
                    pool.tensor_tensor((tmp, tmu)[n % 2][:], AT[:], four(negmt[n]), ALU.mult).then_inc(sem("a_level"), 1)
            pool.wait_ge(sem("m_lo"), 8)
            pool.dma_start(res[:], A["x"][0].rearrange("(t p) n -> p t n", p=P)).then_inc(sem("res_in"), 16)
            pool.dma_start(lng[:], A["ln_mix_g"][0].partition_broadcast(P)).then_inc(sem("ln1_in"), 16)
            pool.dma_start(lnb[:], A["ln_mix_b"][0].partition_broadcast(P)).then_inc(sem("ln1_in"), 16)
            pool.dma_start(pb[:], A["b_ple_gate"][0].partition_broadcast(P)).then_inc(sem("pb_in"), 16)
            pool.wait_ge(sem("quarter_done"), 4 * U_DOWN)
            pool.dma_start(lng2[:], A["ln_ffn_g"][0].partition_broadcast(P)).then_inc(sem("ln2_in"), 16)
            pool.dma_start(lnb2[:], A["ln_ffn_b"][0].partition_broadcast(P)).then_inc(sem("ln2_in"), 16)

        @block.tensor
        def _(pe):
            def cols_quarter(pos, n, j, bank, mh, ml):
                pe.wait_ge(sem("lo_ready"), pos.val(n + 1))
                s = pos.slot(n)
                for kk in range(2):
                    k = 2 * j + kk
                    for f in range(2):
                        wh = hi[:, s, kk * 256 + f * P:kk * 256 + f * P + P]
                        wl = lo[:, s, kk * 256 + f * P:kk * 256 + f * P + P]
                        o = dense[:, bank + f, 0:T]
                        pe.matmul(o, wh, mh[:, k, :], start=(k == 0), stop=False)
                        pe.matmul(o, wh, ml[:, k, :], start=False, stop=False)
                        mm = pe.matmul(o, wl, mh[:, k, :], start=False, stop=(k == KT - 1))
                mm.then_inc(sem("quarter_done"), 1)

            def rows_quarter(pos, n, k, nk, bank, sh, sl):
                pe.wait_ge(sem("lo_ready"), pos.val(n + 1))
                s = pos.slot(n)
                for t in range(TT):
                    o = dense[:, bank + t, :]
                    ah, al = sh[:, k, t * P:t * P + P], sl[:, k, t * P:t * P + P]
                    pe.matmul(o, ah, hi[:, s, :], start=(k == 0), stop=False)
                    pe.matmul(o, al, hi[:, s, :], start=False, stop=False)
                    mm = pe.matmul(o, ah, lo[:, s, :], start=False, stop=(k == nk - 1))
                mm.then_inc(sem("quarter_done"), 1)

            pe.wait_ge(sem("cst_in"), 16)
            for b in range(8):
                if b == 0:
                    for t in range(TT):
                        pe.wait_ge(sem(f"x_in{t}"), 16)
                if b >= 4:
                    pe.wait_ge(sem("x_lo"), b - 3)
                for k in range(2):
                    for t in range(TT):
                        tr = pe.transpose(C[:, b % 4, (2 * k + t) * P:(2 * k + t) * P + P],
                                          xrow[:, t, (2 * b + k) * P:(2 * b + k) * P + P], ident)
                tr.then_inc(sem("x_cols"), 1)
            pe.wait_ge(sem("wdb_lo"), due("wdb_lo"))
            pe.wait_ge(sem("x_lo"), 8)
            for t in range(TT):
                for k in range(KT):
                    o = C[:, 0, 32 * t:32 * t + 32]
                    ah, al = xh[:, k, t * P:t * P + P], xl[:, k, t * P:t * P + P]
                    pe.matmul(o, ah, wdbh[:, k, :], start=(k == 0), stop=False)
                    pe.matmul(o, al, wdbh[:, k, :], start=False, stop=False)
                    mm = pe.matmul(o, ah, wdbl[:, k, :], start=False, stop=(k == KT - 1))
            mm.then_inc(sem("dbda"), 1)
            pe.wait_ge(sem("rows_in"), 80)
            pe.transpose(C[:, 1, 0:97], rowsA[0:97, 0, :], cst[0:97, C_IDENT:C_IDENT + 97])
            pe.transpose(C[:, 1, 128:256], rowsA[:, 1, :], ident)
            pe.transpose(C[:, 2, 0:64], rowsA[0:64, 2, :], cst[0:64, C_IDENT:C_IDENT + 64])
            pe.wait_ge(sem("p_in"), 16)
            for k in range(2):
                for t in range(TT):
                    tr = pe.transpose(C[:, 3, (2 * k + t) * P:(2 * k + t) * P + P], prow[:, t, k * P:k * P + P], ident)
            tr.then_inc(sem("set_cols"), 1)
            for j in range(16):
                rows_quarter(Pos(0), j, j, 16, 0, xh, xl)
            pe.wait_ge(sem("graw"), due("graw"))
            pe.wait_ge(sem("cst2_in"), 16)
            pe.wait_ge(sem("p_lo"), due("p_lo"))
            for t in range(TT):
                r = graw[:, t, :]
                pe.matmul(C[:, 0, 16 * t:16 * t + 16], cst[:, C_CUM:C_CUM + P], r, start=True, stop=True)
                pe.matmul(C[:, 0, 32 + 16 * t:48 + 16 * t], cst2[:, 0:P], r, start=True, stop=True)
                for b in range(2):
                    c = 2 * t + b
                    mm = pe.matmul(C[:, 0, 64 + 16 * c:80 + 16 * c], cst2[:, P + P * b:2 * P + P * b], r,
                                   start=True, stop=True)
            mm.then_inc(sem("gsums"), 1)

            with pe.Fori(0, 2) as m:
                for e in range(2):
                    if e == 1:
                        pe.wait_ge(sem("rows_out"), 2 * m + 1)
                    for j in range(16):
                        rows_quarter(Pos(16 + 16 * e, 32, m), j, j, 16, 2 * ((1 + e) % 2), xh, xl)
                pe.wait_ge(sem("rows_out"), 2 * m + 2)
            pe.wait_ge(sem("k_rot"), due("k_rot"))
            for g in range(KV):
                for t in range(TT):
                    tr = pe.transpose(C[:, 1 + g // 2, (2 * (g % 2) + t) * P:(2 * (g % 2) + t) * P + P],
                                      krot[:, t, g].rearrange("p a d -> p (a d)"), ident)
            tr.then_inc(sem("k_cols"), 1)

            def blk(m, x):
                return m[:, x, :]

            def norms(p):
                pe.wait_ge(sem("sqk"), p + 1)
                pe.matmul(C[:, 0, :], ones, flat(kh[:]), start=True, stop=True).then_inc(sem("ss_k"), 1)
                pe.wait_ge(sem("sqq"), p + 1)
                pe.matmul(C[:, 1, :], ones, flat(qh[:]), start=True, stop=True).then_inc(sem("ss_q"), 1)
                pe.wait_ge(sem("gl"), p + 1)
                pe.matmul(C[:, 2, :], ones, flat(Ym[:]), start=True, stop=True).then_inc(sem("G"), 1)

            def v_to_rows(p):
                pe.wait_ge(sem("silv"), p + 1)
                for h in range(2):
                    for t in range(TT):
                        tr = pe.transpose(C[:, 3, (2 * h + t) * P:(2 * h + t) * P + P], cv[:, h, t * P:t * P + P], ident)
                tr.then_inc(sem("v_rows"), 1)

            def kk_qk(p):
                pe.wait_ge(sem("khat"), p + 1)
                for x in range(4):
                    c = slice((x % 2) * P, (x % 2) * P + P)
                    mm = pe.matmul(C[:, 0, x * P:x * P + P], kh[:, x // 2, c], kh[:, x // 2, c], start=True, stop=True)
                mm.then_inc(sem("KK"), 1)
                pe.wait_ge(sem("qhat"), p + 1)
                for x in range(4):
                    c = slice((x % 2) * P, (x % 2) * P + P)
                    mm = pe.matmul(C[:, 1, x * P:x * P + P], qh[:, x // 2, c], kh[:, x // 2, c], start=True, stop=True)
                mm.then_inc(sem("QKp"), 1)

            def k_to_rows(p):
                pe.wait_ge(sem("bv"), p + 1)
                for h in range(2):
                    for t in range(TT):
                        tr = pe.transpose(C[:, 3, (2 * h + t) * P:(2 * h + t) * P + P], kh[:, h, t * P:t * P + P], ident)
                tr.then_inc(sem("k_rows"), 1)

            def turn_masks(p):
                pe.wait_ge(sem("A"), p + 1)
                for x in range(4):
                    tr = pe.transpose(C[:, 0, x * P:x * P + P], Am[:, x, :], ident)
                tr.then_inc(sem("A_t"), 1)
                pe.wait_ge(sem("QKm"), p + 1)
                for x in range(4):
                    tr = pe.transpose(C[:, 1, x * P:x * P + P], QK[:, x, :], ident)
                tr.then_inc(sem("QK_t"), 1)

            def inv_y(p, n):
                pe.wait_ge(sem("a_level"), nth("a_level", n, p))
                pe.wait_ge(sem("inverse"), nth("inverse", n - 1, p))
                for x in range(4):
                    mm = pe.matmul(C[:, 2, x * P:x * P + P], (tmp, tmu)[n % 2][:, x, :], Tm[:, x, :], start=True, stop=True)
                mm.then_inc(sem("y_prod"), 1)

            def inv_x(p, n):
                pe.wait_ge(sem("y_out"), nth("y_out", n, p))
                pe.wait_ge(sem("inverse_t"), nth("inverse_t", n - 1, p))
                if n < 5:
                    for x in range(4):
                        mm = pe.matmul(C[:, 0, x * P:x * P + P], Um[:, x, :], Ym[:, x, :], start=True, stop=True)
                    mm.then_inc(sem("x_prod"), 1)
                for x in range(4):
                    mm = pe.matmul(C[:, 1, x * P:x * P + P], Ym[:, x, :], Um[:, x, :], start=True, stop=True)
                mm.then_inc(sem("xt_prod"), 1)

            def scan_ks(p, c):
                b, R = c % 2, slice(CH * (c % 2), CH * (c % 2) + CH)
                pe.wait_ge(sem("state"), nth("state", c - 1, p))
                for h in range(2):
                    mm = pe.matmul(C[R, 1, h * P:h * P + P], kh[:, h, CH * c:CH * c + CH], S[:, h, :], start=True, stop=True)
                mm.then_inc(sem("ks_prod"), 1)

            def scan_v(p, c):
                R = slice(CH * (c % 2), CH * (c % 2) + CH)
                if c == 0:
                    pe.wait_ge(sem("inverse_t"), nth("inverse_t", 5, p))
                else:
                    pe.wait_ge(sem("rhs"), nth("rhs", c, p))
                for h in range(2):
                    x = 2 * h + c // 2
                    mm = pe.matmul(C[R, 2, h * P:h * P + P], Um[:, x, CH * (c % 2):CH * (c % 2) + CH],
                                   bv[:, x, :] if c == 0 else rr[:, h, :], start=True, stop=True)
                mm.then_inc(sem("v_prod"), 1)

            def scan_o(p, c, att):
                b, R = c % 2, slice(CH * (c % 2), CH * (c % 2) + CH)
                pe.wait_ge(sem("v_out"), nth("v_out", c, p))
                if c == 0:
                    pe.wait_ge(sem("QKTc"), p + 1)
                if c == 0 and att:
                    pe.wait_ge(sem("att_out"), p + 2)
                for h in range(2):
                    x = 2 * h + c // 2
                    o = C[:, 3, h * T + CH * c:h * T + CH * c + CH]
                    if c:
                        pe.matmul(o, S[:, h, :], qd[:, h, CH * c:CH * c + CH], start=True, stop=False)
                    mm = pe.matmul(o, vn[R, h, :], QKT[R, x, CH * b:CH * b + CH], start=(c == 0), stop=True)
                if c < 3:
                    for h in range(2):
                        x = 2 * h + c // 2
                        mm = pe.matmul(C[:, 0, h * P:h * P + P], kd[R, x, :], vn[R, h, :], start=True, stop=True)
                mm.then_inc(sem("o_prod"), 1)

            def o_norm(p):
                pe.wait_ge(sem("sqo"), p + 1)
                pe.matmul(C[:, 1, :], ones, flat(tmp[:]), start=True, stop=True).then_inc(sem("ss_o"), 1)

            def att_q(i, chain):
                if chain:
                    pe.wait_ge(sem("kdec"), i)
                pe.wait_ge(sem("qrot"), i + 1)
                for u in range(4):
                    tr = pe.transpose(C[:, 3, u * P:u * P + P], qr[:].rearrange("p h d -> p (h d)")[:, u * P:u * P + P], ident)
                tr.then_inc(sem("q_cols"), 1)

            def att_scores(i, n, b):
                if b == 0:
                    pe.wait_ge(sem("qTc"), i + 1) if n == 0 else pe.wait_ge(sem("sE"), i + 1)
                    if n == 0:
                        pe.wait_ge(sem("kvS"), i + 1)
                else:
                    pe.wait_ge(sem(f"sc{n}0"), i + 1)
                R = slice(64 * b, 64 * b + 64)
                for j in range(2):
                    r = 2 * b + j
                    mm = pe.matmul(C[:, 3, r * P:r * P + P], qT[R, n, 2 * j:2 * j + 2, :].rearrange("p a c -> p (a c)"),
                                   kS[R, CH * n:CH * n + P], start=True, stop=True)
                mm.then_inc(sem(f"sc{n}{b}"), 1)

            def att_turn(i, n):
                pe.wait_ge(sem("prob0" if n == 0 else "prob1"), i + 1)
                if n == 1:
                    pe.wait_ge(sem("pTE"), i + 1)
                m = sE if n == 0 else sO
                for r in range(4):
                    tr = pe.transpose(C[:, 3, r * P:r * P + P], m[:, r, :], ident)
                tr.then_inc(sem(f"pt{n}"), 1)

            def att_pv(i):
                pe.wait_ge(sem("pTO"), i + 1)
                for n in range(2):
                    m = pTE if n == 0 else pTO
                    for b in range(2):
                        mm = pe.matmul(C[64 * b:64 * b + 64, 3, n * T:n * T + T], vS[:, n, :], m[:, b * T:b * T + T],
                                       start=True, stop=True)
                mm.then_inc(sem("pv"), 1)

            def chain_stage(k, p, att):
                if k == NORMS - LAG:
                    norms(p)
                elif k == 1:
                    v_to_rows(p)
                elif k == 2:
                    kk_qk(p)
                elif k == 3:
                    k_to_rows(p)
                elif k == 4:
                    turn_masks(p)
                elif k in (5, 7, 9, 11, 13):
                    inv_y(p, (k - 3) // 2)
                elif k in (6, 8, 10, 12, 14):
                    inv_x(p, (k - 4) // 2)
                elif k in (17, 20, 23):
                    scan_ks(p, (k - 14) // 3)
                elif k in (15, 18, 21, 24):
                    scan_v(p, (k - 15) // 3)
                elif k in (16, 19, 22, 25):
                    scan_o(p, (k - 16) // 3, att)
                elif k == 26:
                    o_norm(p)

            def att_stage(k, i, chain):
                if k == 5:
                    att_q(i, chain)
                elif k in (6, 7, 8, 9):
                    att_scores(i, (k - 6) // 2, k % 2)
                elif k == 13:
                    att_turn(i, 0)
                elif k == 14:
                    att_turn(i, 1)
                elif k == 15:
                    att_pv(i)

            def mixer_turn(i, chain):
                pos = Pos(4 * U_LOOP, 32, i)
                for k in range(32):
                    s = k // 8
                    if k % 8 == 0:
                        if s == 0 and chain:
                            pe.wait_ge(sem("pad2"), i)
                        elif s == 1:
                            pe.wait_ge(sem("z_in"), i) if chain else pe.wait_ge(sem("rows_out"), 5)
                        elif s == 2:
                            pe.wait_ge(sem("pad0"), i + 1)
                        elif s == 3:
                            pe.wait_ge(sem("pad1"), i + 1)
                    cols_quarter(pos, k, k % 8, 2 * ((s + 1) % 2), xh, xl)
                    if chain:
                        chain_stage(k - LAG, i - 1, True)
                    att_stage(k - LAG, i, chain)

            mixer_turn(0, False)
            with pe.Fori(1, PAIRS) as i:
                mixer_turn(i, True)
            for k in range(NORMS - LAG, 30):
                chain_stage(k, PAIRS - 1, False)
                if k == 0:
                    pe.wait_ge(sem("pad2"), PAIRS)
                if k in TAIL:
                    cols_quarter(Pos(4 * U_YA), TAIL.index(k), TAIL.index(k), 2, xh, xl)

            def branch(pos, j, lo_base, prev, start=0):
                for k in range(start, 16):
                    if k == 0 and prev[0] is not None:
                        pe.wait_ge(sem(prev[0][0]), prev[0][1])
                    if k == 8 and prev[1] is not None:
                        pe.wait_ge(sem(prev[1][0]), prev[1][1])
                    g = k // 8
                    if g == 1:
                        if lo_base is not None:
                            pe.wait_ge(sem("b_lo"), lo_base + k - 7)
                        cols_quarter(pos, k, k - 8, 0, bh, bl)
                    else:
                        cols_quarter(pos, k, k, 2, xh, xl)

            branch(Pos(4 * U_YA, 16, 0), 0, 0, (None, ("z_in", PAIRS)), start=8)
            with pe.Fori(1, 8) as j:
                branch(Pos(4 * U_YA, 16, j), j, None, (("gate", j), ("prod", j)))
            branch(Pos(4 * U_YD, 16, 0), 0, 8, (("gate", 8), ("prod", 8)))
            with pe.Fori(1, 8) as j:
                branch(Pos(4 * U_YD, 16, j), j, None, (("gate", j + 8), ("prod", j + 8)))

            pe.wait_ge(sem("gate"), 16)
            for c in range(4):
                if c == 1:
                    pe.wait_ge(sem("prod"), 16)
                elif c >= 2:
                    pe.wait_ge(sem("mix_out"), c - 1)
                for k in range(16):
                    if c == 0 and k % 2 == 0:
                        pe.wait_ge(sem("m_lo"), k // 2 + 1)
                    rows_quarter(Pos(4 * U_OUT), 16 * c + k, k, 16, 2 * ((c + 1) % 2), xh, xl)
            def p_product(pos):
                for n in range(4):
                    pe.wait_ge(sem("lo_ready"), pos.val(n + 1))
                    s = pos.slot(n)
                    for t in range(TT):
                        o = C[:, 2 * (n % 2) + t, :]
                        a, b = ph[:, n // 2, t * P:t * P + P], pl[:, n // 2, t * P:t * P + P]
                        pe.matmul(o, a, hi[:, s, :], start=(n < 2), stop=False)
                        pe.matmul(o, b, hi[:, s, :], start=False, stop=False)
                        mm = pe.matmul(o, a, lo[:, s, :], start=False, stop=(n >= 2))
                    mm.then_inc(sem("quarter_done"), 1)

            p_product(Pos(4 * U_PLE))
            for b in range(8):
                if b % 2 == 0:
                    pe.wait_ge(sem("h1_rows"), b + 2)
                if b >= 4:
                    pe.wait_ge(sem("h1_lo"), b - 3)
                for k in range(2):
                    for t in range(TT):
                        tr = pe.transpose(dense[:, b % 4, (2 * k + t) * P:(2 * k + t) * P + P],
                                          res[:, t, (2 * b + k) * P:(2 * b + k) * P + P], ident)
                tr.then_inc(sem("h1_cols"), 1)
            pe.wait_ge(sem("h1_lo"), 8)
            for g in range(4):
                if g == 3:
                    pe.wait_ge(sem("ple_out"), 2)
                    p_product(Pos(4 * U_PLE + P_AT[1]))
                if g >= 2:
                    pe.wait_ge(sem("pgate"), g - 1)
                for k in range(16):
                    rows_quarter(Pos(4 * U_PLE), GATE_AT[g] + k, k, 16, 2 * ((g + 1) % 2), xh, xl)

            def ffn_turn(f, first):
                for k in range(16):
                    if k == 0:
                        pe.wait_ge(sem("pgate"), 3) if first else pe.wait_ge(sem("ff_gate"), f)
                    if k == 8:
                        pe.wait_ge(sem("pgate"), 4) if first else pe.wait_ge(sem("ff_prod"), f)
                    cols_quarter(Pos(4 * U_FFN, 16, f), k, k % 8, 2 if k < 8 else 0, xh, xl)
            ffn_turn(0, True)
            with pe.Fori(1, FF // 256) as f:
                ffn_turn(f, False)

            for c in range(4):
                if c == 0:
                    pe.wait_ge(sem("ff_gate"), FF // 256)
                elif c == 1:
                    pe.wait_ge(sem("ff_prod"), FF // 256)
                else:
                    pe.wait_ge(sem("down_out"), c - 1)
                for k in range(FT):
                    if c == 0:
                        pe.wait_ge(sem("hid_lo"), k // 2 + 1)
                    rows_quarter(Pos(4 * U_DOWN), FT * c + k, k, FT, 2 * ((c + 1) % 2), hh, hl)

        @block.scalar
        def _(act):
            def split(pos, n):
                slot, val = pos.raw(n)
                if (pos.q + n) % 4 == 0:
                    act.wait_ge(sem(f"raw_in{slot}"), val)
                if pos.q + n >= RING:
                    act.wait_ge(sem("quarter_done"), pos.val(n - RING + 1))
                off = ((pos.q + n) % 4) * 512
                act.activation(hi[:, pos.slot(n), :], raw[:, slot, off:off + 512],
                               ACT.Copy).then_inc(sem("hi_ready"), 1)

            act.wait_ge(sem("wdb_in"), 16)
            act.activation(wdbh[:], wdb[:], ACT.Copy).then_inc(sem("wdb_hi"), 1)
            for b in range(8):
                act.wait_ge(sem("x_cols"), b + 1)
                act.activation(flat(xh[:, 2 * b:2 * b + 2, :]), C[:, b % 4, :], ACT.Copy).then_inc(sem("x_hi"), 1)
            for n in range(LEAD):
                split(Pos(0), n)
            act.wait_ge(sem("g_in"), 48)
            act.activation(st[:, 0, 0, :], gbias[:, 32:48], ACT.Exp).then_inc(sem("ealog"), 1)
            act.wait_ge(sem("set_cols"), due("set_cols"))
            act.activation(bcol[:], C[:, 1, 0:97], ACT.Copy).then_inc(sem("bcol"), 1)
            act.activation(flat(ph[:]), C[:, 3, :], ACT.Copy, scale=0.5).then_inc(sem("p_hi"), 1)
            for j in range(16):
                split(Pos(LEAD), j)
                if j == 3:
                    act.wait_ge(sem("dbda_rows"), due("dbda_rows"))
                    act.activation(st[:, 1], dbda[:, :, 0:16], ACT.Exp, scale=-1.0).then_inc(sem("eneg"), 1)
                    act.wait_ge(sem("dt_sum"), due("dt_sum"))
                    act.activation(st[:, 3], st[:, 2], ACT.Abs).then_inc(sem("yabs"), 1)
                    act.wait_ge(sem("yabs"), due("yabs"))
                    act.activation(st[:, 4], st[:, 3], ACT.Exp, scale=-1.0).then_inc(sem("eabs"), 1)
            with act.Fori(0, 2) as m:
                for e in range(2):
                    for j in range(16):
                        split(Pos(16 + 16 * e + LEAD, 32, m), j)
            act.wait_ge(sem("gsums_out"), due("gsums_out"))
            act.activation(st[:, 5], gcol[:], ACT.Exp).then_inc(sem("eg"), 1)
            act.activation(kdecs[:], st[:, 6], ACT.Exp).then_inc(sem("kdecs"), 1)
            act.activation(dall[:].rearrange("p c h -> p (c h)"), C[:, 0, 64:128], ACT.Exp).then_inc(sem("dall"), 1)
            act.wait_ge(sem("k_cols"), due("k_cols"))
            act.wait_ge(sem("k_zero"), 1)
            for g in range(KV):
                c0 = (g % 2) * T
                act.activation(kTall[:, 2 * g, 64:192], C[:, 1 + g // 2, c0:c0 + 128],
                               ACT.Copy).then_inc(sem("kT_out"), 1)
                act.activation(kTall[:, 2 * g + 1, :], C[:, 1 + g // 2, c0 + 64:c0 + 256],
                               ACT.Copy).then_inc(sem("kT_out"), 1)

            def pad_in(i, s):
                for f in range(2):
                    if f == 0:
                        act.wait_ge(sem("quarter_done"), 4 * U_LOOP + 8 * (s + 1) + 32 * i)
                        if s:
                            act.wait_ge(sem(f"conv{s - 1}"), 2 * i + 2)
                        elif not isinstance(i, int):
                            act.wait_ge(sem("conv2"), 2 * i)
                        else:
                            act.wait_ge(sem("pad_zero"), due("pad_zero"))
                    r = act.activation(pad[:, f, 3:T + 3], dense[:, 2 * ((s + 1) % 2) + f, 0:T], ACT.Identity,
                                       bias=bcol[:, ds(16 * s + f + 2 * i, 1)])
                r.then_inc(sem(f"pad{s}"), 1)

            def qk_front(k, i):
                if k == 26:
                    act.wait_ge(sem("conv0"), 2 * i + 2)
                    act.activation(flat(AT[:]), flat(cq[:]), ACT.Tanh, scale=0.5).then_inc(sem("tanh"), 1)
                elif k == 27:
                    act.wait_ge(sem("conv1"), 2 * i + 2)
                    act.activation(flat(Am[:]), flat(ck[:]), ACT.Tanh, scale=0.5).then_inc(sem("tanh"), 1)
                elif k == 30:
                    act.wait_ge(sem("silk"), i + 1)
                    act.activation(flat(kh[:]), flat(ck[:]), ACT.Square).then_inc(sem("sqk"), 1)
                    act.wait_ge(sem("silq"), i + 1)
                    act.activation(flat(qh[:]), flat(cq[:]), ACT.Square, scale=float(P) ** 0.5).then_inc(sem("sqq"), 1)

            def chain_k(k, p):
                if k == 0:
                    act.wait_ge(sem("quarter_done"), 4 * U_LOOP + 32 + 32 * p)
                    for f in range(2):
                        r = act.activation(zb[:, f, :], dense[:, f, 0:T], ACT.Identity,
                                           bias=bcol[:, ds(48 + f + 2 * p, 1)])
                    r.then_inc(sem("z_in"), 1)
                    act.wait_ge(sem("conv2"), 2 * p + 2)
                    act.activation(flat(Tm[:]), flat(cv[:]), ACT.Tanh, scale=0.5).then_inc(sem("tanh"), 1)
                    act.wait_ge(sem("z_in"), p + 1)
                    act.activation(flat(Um[:]), flat(zb[:]), ACT.Tanh, scale=0.5).then_inc(sem("tanh"), 1)
                elif k == "norms":
                    act.wait_ge(sem("ss_k"), p + 1)
                    act.activation(flat(kh[:]), C[:, 0, :], ACT.Ln, bias=eps_k).then_inc(sem("lnk"), 1)
                    act.wait_ge(sem("ss_q"), p + 1)
                    act.activation(flat(qh[:]), C[:, 1, :], ACT.Ln, bias=eps_q).then_inc(sem("lnq"), 1)
                    act.wait_ge(sem("lnk"), p + 1)
                    act.activation(flat(kh[:]), flat(kh[:]), ACT.Exp, scale=-0.5).then_inc(sem("rnk"), 1)
                    act.wait_ge(sem("lnq"), p + 1)
                    act.activation(flat(qh[:]), flat(qh[:]), ACT.Exp, scale=-0.5).then_inc(sem("rnq"), 1)
                elif k == 2:
                    act.wait_ge(sem("am"), p + 1)
                    act.wait_ge(sem("silq"), p + 1)
                    for x in range(4):
                        h, t = x // 2, x % 2
                        r = act.activation(AT[:, x, :], Am[:, x, :], ACT.Exp, bias=gcol[:, t, ds(h + 2 * p, 1)], scale=-1.0)
                    r.then_inc(sem("E"), 1)
                    act.activation(flat(egb[:]), C[:, 2, :], ACT.Exp).then_inc(sem("egb"), 1)
                elif k == 4:
                    act.wait_ge(sem("A_t"), p + 1)
                    act.activation(flat(AT[:]), C[:, 0, :], ACT.Copy).then_inc(sem("ATc"), 1)
                    act.wait_ge(sem("QK_t"), p + 1)
                    act.activation(flat(QKT[:]), C[:, 1, :], ACT.Copy).then_inc(sem("QKTc"), 1)
                elif k in (15, 18, 21, 24):
                    c = (k - 15) // 3
                    R = slice(CH * (c % 2), CH * (c % 2) + CH)
                    act.wait_ge(sem("v_prod"), nth("v_prod", c, p))
                    act.activation(vn[R, :, :].rearrange("p a b -> p (a b)"), C[R, 2, 0:256],
                                   ACT.Copy).then_inc(sem("v_out"), 1)
                    if c == 3:
                        act.wait_ge(sem("o_prod"), nth("o_prod", 3, p))
                        act.activation(flat(tmp[:]), C[:, 3, :], ACT.Square,
                                       scale=float(P) ** -0.5).then_inc(sem("sqo"), 1)
                elif k == 27:
                    act.wait_ge(sem("ss_o"), p + 1)
                    act.activation(flat(tmu[:]), C[:, 1, :], ACT.Ln, bias=eps_o).then_inc(sem("lno"), 1)
                    act.wait_ge(sem("lno"), p + 1)
                    act.activation(flat(tmu[:]), flat(tmu[:]), ACT.Exp, scale=-0.5).then_inc(sem("rno"), 1)

            def y_copy(k, p):
                if k in (5, 7, 9, 11, 13):
                    act.wait_ge(sem("y_prod"), nth("y_prod", (k - 3) // 2, p))
                    act.activation(flat(Ym[:]), C[:, 2, :], ACT.Copy).then_inc(sem("y_out"), 1)

            def att_k(k, i):
                if k == 6:
                    act.wait_ge(sem("q_cols"), i + 1)
                    act.activation(qT[:].rearrange("p n u c -> p u n c"),
                                   C[:, 3, :].rearrange("p (u n c) -> p u n c", u=4, n=2),
                                   ACT.Copy).then_inc(sem("qTc"), 1)
                elif k == 10:
                    act.wait_ge(sem("sc11"), i + 1)
                    act.activation(flat(sO[:]), C[:, 3, :], ACT.Copy).then_inc(sem("sO"), 1)
                elif k in (11, 12):
                    n = k - 11
                    m = (sE, sO)[n]
                    act.wait_ge(sem("nmax"), i + 1)
                    for r in range(4):
                        q = 4 * n + r
                        a = act.activation(m[:, r, :], m[:, r, :], ACT.Exp, bias=sm[:, 2, q:q + 1], scale=ATT_SCALE,
                                           accum_out=sm[:, 4, q:q + 1])
                    if n == 0:
                        act.activation(sm[:, 5, :], sm[:, 3, :], ACT.Exp).then_inc(sem("exp0"), 1)
                    else:
                        a.then_inc(sem("exp1"), 1)
                elif k == 13:
                    act.wait_ge(sem("pt0"), i + 1)
                    act.activation(pTE[:], C[:, 3, :], ACT.Copy).then_inc(sem("pTE"), 1)
                elif k == 14:
                    act.wait_ge(sem("pt1"), i + 1)
                    act.activation(pTO[:], C[:, 3, :], ACT.Copy).then_inc(sem("pTO"), 1)
                elif k == 15:
                    act.wait_ge(sem("pv"), i + 1)
                    act.activation(qbuf[:, ds(i, 1), :].rearrange("p o (u n c) -> p (o u) n c", u=4, n=2),
                                   C[:, 3, :].rearrange("p (n u c) -> p u n c", n=2, u=4),
                                   ACT.Copy).then_inc(sem("att_out"), 1)

            def mixer_turn(i, chain):
                pos = Pos(4 * U_LOOP + LEAD, 32, i)
                for k in range(32):
                    split(pos, k)
                    if chain:
                        if k == 0:
                            chain_k(0, i - 1)
                        elif k > LAG:
                            chain_k(k - LAG, i - 1)
                            y_copy(k - LAG, i - 1)
                        if k == NORMS:
                            chain_k("norms", i - 1)
                        if k == 31:
                            act.wait_ge(sem("on"), i)
                    att_k(k - LAG, i)
                    qk_front(k, i)
                    if k == 9:
                        pad_in(i, 0)
                    elif k == 17:
                        pad_in(i, 1)
                    elif k == 25:
                        pad_in(i, 2)

            eps_k, eps_q, eps_o = epsc[:, 0:1], epsc[:, 1:2], epsc[:, 2:3]
            mixer_turn(0, False)
            with act.Fori(1, PAIRS) as i:
                mixer_turn(i, True)
            for k in range(30):
                chain_k(k, PAIRS - 1)
                y_copy(k, PAIRS - 1)
                if k == 0:
                    chain_k("norms", PAIRS - 1)
                if k in TAIL:
                    split(Pos(4 * U_YA + LEAD), TAIL.index(k))

            def gates(pos, j, b0, gt_used, start=0):
                for k in range(16):
                    if k >= start:
                        split(pos, k)
                    if k == 8 - 1:
                        act.wait_ge(sem("quarter_done"), pos.val(8 - LEAD))
                        if gt_used is not None:
                            act.wait_ge(sem(gt_used[0]), gt_used[1])
                        for f in range(2):
                            r = act.activation(gt[:, 0, f, :], dense[:, 2 + f, 0:T], ACT.Tanh,
                                               bias=hbias[:, ds(b0 + f + 2 * j, 1)], scale=0.5)
                        r.then_inc(sem("gate"), 1)

            act.wait_ge(sem("on"), 8)
            for b in range(8):
                m = bh[:, 2 * b:2 * b + 2, :]
                act.activation(m.rearrange("p u (t c) -> p u t c", t=TT), att_cols(b),
                               ACT.Copy).then_inc(sem("b_hi"), 1)
            gates(Pos(4 * U_YA + LEAD, 16, 0), 0, 0, None, start=8)
            with act.Fori(1, 8) as j:
                gates(Pos(4 * U_YA + LEAD, 16, j), j, 0, ("prod", j))
            act.wait_ge(sem("quarter_done"), 4 * U_YD)
            for b in range(8):
                act.activation(flat(bh[:, 2 * b:2 * b + 2, :]), flat(odn[:, 2 * b:2 * b + 2, :]),
                               ACT.Copy).then_inc(sem("b_hi"), 1)
            gates(Pos(4 * U_YD + LEAD, 16, 0), 0, 16, ("prod", 8))
            with act.Fori(1, 8) as j:
                gates(Pos(4 * U_YD + LEAD, 16, j), j, 16, ("prod", j + 8))
            act.wait_ge(sem("prod"), 16)
            act.wait_ge(sem("quarter_done"), 4 * U_OUT)
            for b in range(8):
                act.activation(flat(xh[:, 2 * b:2 * b + 2, :]), flat(merged[:, 2 * b:2 * b + 2, :]), ACT.Copy,
                               scale=0.5).then_inc(sem("m_hi"), 1)
            for k in range(64):
                split(Pos(4 * U_OUT + LEAD), k)

            def norm_scale(which, t):
                act.wait_ge(sem("variance"), 2 * which + t - 1)
                act.activation(lnst_of[which][:, t, 26:27], lnst_of[which][:, t, 25:26], ACT.Sqrt,
                               bias=eps_ln).then_inc(sem("deviation"), 1)

            eps_ln = epsc[:, 3:4]
            for t in range(TT):
                norm_scale(1, t)
            for b in range(8):
                act.wait_ge(sem("h1_cols"), b + 1)
                act.activation(flat(xh[:, 2 * b:2 * b + 2, :]), dense[:, b % 4, :], ACT.Copy).then_inc(sem("h1_hi"), 1)

            for n in range(72):
                split(Pos(4 * U_PLE + LEAD), n)
                if n in (20, 36, 52, 71):
                    g = (20, 36, 52, 71).index(n)
                    act.wait_ge(sem("pgate"), g + 1)
                    act.activation(flat(pg[:, g % 2]), flat(pg[:, g % 2]), ACT.Tanh,
                                   scale=0.5).then_inc(sem("ptanh"), 1)

            def ffn_turn(f, n):
                pos = Pos(4 * U_FFN + LEAD, 16, f)
                for k in range(n):
                    split(pos, k)
                    if k == 7:
                        act.wait_ge(sem("quarter_done"), 4 * U_FFN + 8 + 16 * f)
                        if not isinstance(f, int) or f > 0:
                            act.wait_ge(sem("ff_prod"), f)
                        act.activation(ff[:, 0], dense[:, 2:4, 0:T], ACT.Silu).then_inc(sem("ff_gate"), 1)
                    if k == 15:
                        act.wait_ge(sem("ff_prod"), f + 1)
                        act.activation(hh[:, ds(2 * f, 2), :], ff[:, 1], ACT.Copy).then_inc(sem("hid_hi"), 1)

            ffn_turn(0, 16)
            with act.Fori(1, FF // 256 - 1) as f:
                ffn_turn(f, 16)
            ffn_turn(FF // 256 - 1, 16)
            for n in range(4 * FT - LEAD):
                split(Pos(4 * U_DOWN + LEAD), n)
            for t in range(TT):
                norm_scale(2, t)

        @block.vector
        def _(dve):
            def split(pos, n):
                slot = pos.raw(n)[0]
                dve.wait_ge(sem("hi_ready"), pos.val(n + 1))
                off = ((pos.q + n) % 4) * 512
                dve.tensor_tensor(lo[:, pos.slot(n), :], raw[:, slot, off:off + 512],
                                  hi[:, pos.slot(n), :].bitcast(F32), ALU.subtract).then_inc(sem("lo_ready"), 1)

            steps = {}

            def own(kind):
                steps[kind] = steps.get(kind, 0) + 1
                return kind

            for k, v in enumerate((4 * L2_EPS, P * 4 * L2_EPS, RMS_EPS, LN_EPS)):
                dve.memset(epsc[:, k:k + 1], v)
            dve.wait_ge(sem("wdb_hi"), due("wdb_hi"))
            dve.tensor_tensor(wdbl[:], wdb[:], wdbh[:].bitcast(F32), ALU.subtract).then_inc(sem("wdb_lo"), 1)
            for b in range(8):
                dve.wait_ge(sem("x_hi"), b + 1)
                dve.tensor_tensor(flat(xl[:, 2 * b:2 * b + 2, :]), C[:, b % 4, :],
                                  flat(xh[:, 2 * b:2 * b + 2, :]).bitcast(F32), ALU.subtract).then_inc(sem("x_lo"), 1)
            for n in range(LEAD):
                split(Pos(0), n)
            dve.wait_ge(sem("dbda"), due("dbda"))
            dve.wait_ge(sem("g_in"), 48)
            dve.tensor_tensor(dbda[:], C[:, 0, 0:64].rearrange("p (t n) -> p t n", t=TT),
                              gbias[:, 0:32].unsqueeze(1).to_broadcast([P, TT, 32]),
                              ALU.add).then_inc(sem("dbda_rows"), 1)
            dve.wait_ge(sem("dbda_rows"), due("dbda_rows"))
            dve.tensor_tensor(st[:, 2], dbda[:, :, 16:32], gbias[:, 48:64].unsqueeze(1).to_broadcast([P, TT, 16]),
                              ALU.add).then_inc(sem("dt_sum"), 1)
            dve.wait_ge(sem("bcol"), due("bcol"))
            dve.tensor_scalar(cw[:].rearrange("p j t -> p (j t)")[:, 0:128], C[:, 1, 128:256], 1.0, None, ALU.mult)
            dve.tensor_scalar(cw[:].rearrange("p j t -> p (j t)")[:, 128:192], C[:, 2, 0:64], 1.0, None,
                              ALU.mult).then_inc(sem("taps_in"), 1)
            dve.wait_ge(sem("p_hi"), due("p_hi"))
            dve.scalar_tensor_tensor(flat(pl[:]), C[:, 3, :], 0.5, flat(ph[:]).bitcast(F32), ALU.mult,
                                     ALU.subtract).then_inc(sem("p_lo"), 1)
            dve.tensor_scalar(ghalf[:], bcol[:, 96:97], 0.5, None, ALU.mult)
            dve.tensor_scalar(hbias[:], bcol[:, 64:96], 0.5, None, ALU.mult).then_inc(sem("halves"), 1)
            dve.wait_ge(sem("sink_in"), 16)
            for a in range(2):
                R = slice(64 * a, 64 * a + 64)
                for b in range(2):
                    src = sinkraw[R, :].rearrange("p (g j r) -> p g j r", g=KV, j=2)[:, :, :, 2 * a + b]
                    for r in range(4):
                        dst = sinks[R, :, :].rearrange("p (g t) (n b j) -> p g t n b j", t=TT, n=2, b=2)
                        last = dve.tensor_scalar(dst[:, :, r // 2, r % 2, b, :], src, 1.0, None, ALU.mult)
            last.then_inc(sem("sinks_in"), 1)

            def gates_part(j):
                e, z, z2, acc = st[:, 4], st[:, 6], st[:, 7], st[:, 8]
                if j == 4:
                    dve.wait_ge(sem("eneg"), due("eneg"))
                    dve.tensor_scalar(st[:, 9], st[:, 1], 1.0, None, ALU.add).then_inc(sem(own("setup")), 1)
                    dve.wait_ge(sem("setup"), steps["setup"])
                    dve.reciprocal(beta[:], st[:, 9]).then_inc(sem(own("setup")), 1)
                    dve.wait_ge(sem("setup"), steps["setup"])
                    dve.tensor_scalar(bhalf[:], beta[:], 0.5, None, ALU.mult).then_inc(sem(own("setup")), 1)
                elif j == 5:
                    dve.wait_ge(sem("eabs"), due("eabs"))
                    dve.tensor_scalar(st[:, 9], e, 2.0, None, ALU.add).then_inc(sem(own("setup")), 1)
                    dve.wait_ge(sem("setup"), steps["setup"])
                    dve.reciprocal(st[:, 10], st[:, 9]).then_inc(sem(own("setup")), 1)
                    dve.wait_ge(sem("setup"), steps["setup"])
                    dve.tensor_tensor(z, e, st[:, 10], ALU.mult).then_inc(sem(own("setup")), 1)
                    dve.wait_ge(sem("setup"), steps["setup"])
                    dve.tensor_tensor(z2, z, z, ALU.mult).then_inc(sem(own("setup")), 1)
                    dve.wait_ge(sem("setup"), steps["setup"])
                    dve.tensor_scalar(acc, z2, 2.0 / 19, None, ALU.mult).then_inc(sem(own("setup")), 1)
                elif 6 <= j <= 13:
                    dve.wait_ge(sem("setup"), steps["setup"])
                    dve.scalar_tensor_tensor(acc, acc, 2.0 / (2 * (14 - j) + 1), z2, ALU.add,
                                             ALU.mult).then_inc(sem(own("setup")), 1)
                elif j == 14:
                    dve.wait_ge(sem("setup"), steps["setup"])
                    dve.scalar_tensor_tensor(acc, acc, 2.0, z, ALU.add, ALU.mult).then_inc(sem(own("setup")), 1)
                    dve.wait_ge(sem("setup"), steps["setup"])
                    dve.scalar_tensor_tensor(acc, st[:, 2], 0.0, acc, ALU.max, ALU.add).then_inc(sem(own("setup")), 1)
                    dve.wait_ge(sem("setup"), steps["setup"])
                    dve.wait_ge(sem("ealog"), due("ealog"))
                    dve.scalar_tensor_tensor(graw[:], acc, -1.0, st[:, 0, 0:1, :].to_broadcast([P, TT, HEADS]),
                                             ALU.mult, ALU.mult).then_inc(sem("graw"), 1)

            for j in range(16):
                split(Pos(LEAD), j)
                gates_part(j)

            dve.wait_ge(sem("quarter_done"), 16)
            dve.wait_ge(sem("bq_in"), 16)
            dve.scalar_tensor_tensor(krow[:], dense[:, 0:2, :], 1.0,
                                     biasq[:, AK:AK + 512].unsqueeze(1).to_broadcast([P, TT, 512]), ALU.mult,
                                     ALU.add).then_inc(sem("rows_out"), 1)
            dve.wait_ge(sem("gsums"), due("gsums"))
            dve.tensor_scalar(gcol[:].rearrange("p t h -> p (t h)"), C[:, 0, 0:32], 1.0, None,
                              ALU.mult).then_inc(sem("gcol_in"), 1)
            dve.wait_ge(sem("gcol_in"), due("gcol_in"))
            dve.tensor_tensor(st[:, 6].rearrange("p t h -> p (t h)"), C[:, 0, 32:64],
                              gcol[:].rearrange("p t h -> p (t h)"), ALU.subtract).then_inc(sem("gsums_out"), 1)

            dve.wait_ge(sem("rows_out"), 1)
            dve.wait_ge(sem("v_zero"), 1)
            for t in range(TT):
                q = krow[:, t, 0:256].rearrange("p (h c) -> p h c", c=32)
                cos = cst[:, C_COS + 32 * t:C_COS + 32 * t + 32].unsqueeze(1).to_broadcast([P, 2 * KV, 32])
                sin = cst[:, C_SIN + 32 * t:C_SIN + 32 * t + 32].unsqueeze(1).to_broadcast([P, 2 * KV, 32])
                dve.tensor_tensor(krt[:, t, 0:8], q, cos, ALU.mult).then_inc(sem(own("setup")), 1)
                dve.tensor_tensor(krt[:, t, 8:16], q, sin, ALU.mult).then_inc(sem(own("setup")), 1)
                dve.wait_ge(sem("setup"), steps["setup"])
                tc = krt[:, t, 0:8].rearrange("p (h a) c -> p h a c", a=2)
                ts = krt[:, t, 8:16].rearrange("p (h a) c -> p h a c", a=2)
                for d in range(2):
                    dve.tensor_tensor(krot[:, t, :, d, 0:32], tc[:, :, 0], ts[:, :, 1], ALU.subtract)
                    dve.tensor_tensor(krot[:, t, :, d, 32:64], tc[:, :, 1], ts[:, :, 0], ALU.add)
            dve.tensor_scalar(vall[:, :, 1, :].rearrange("p (g t) d -> p t g d", t=TT),
                              krow[:, :, 256:512].rearrange("p t (g d) -> p t g d", g=KV), 1.0, None,
                              ALU.mult).then_inc(sem("k_rot"), 1)

            with dve.Fori(0, 2) as m:
                for e in range(2):
                    pos = Pos(16 + 16 * e, 32, m)
                    for j in range(16):
                        split(Pos(16 + 16 * e + LEAD, 32, m), j)
                    dve.wait_ge(sem("quarter_done"), pos.val(16))
                    b0 = 2 * ((1 + e) % 2)
                    dve.scalar_tensor_tensor(qbuf[:, ds(4 * m + 2 * e, 2), :], dense[:, b0:b0 + 2, :], 1.0,
                                             biasq[:, ds(1024 * m + 512 * e, 512)].unsqueeze(1).to_broadcast([P, TT, 512]),
                                             ALU.mult, ALU.add).then_inc(sem("rows_out"), 1)
            dve.wait_ge(sem("eg"), due("eg"))
            dve.wait_ge(sem("rows_out"), 5)
            dve.memset(rr[:], 0.0)
            dve.memset(pad[:, :, 0:3], 0.0).then_inc(sem("pad_zero"), 1)
            dve.scalar_tensor_tensor(nbeg[:], st[:, 5], -1.0, beta[:], ALU.mult, ALU.mult).then_inc(sem("nbeg"), 1)

            def conv(i, k):
                n = k - 9
                if not 0 <= n < 24:
                    return
                s, j, f = n // 8, n % 8 // 2, n % 2
                dst = (cq, ck, cv)[s][:, f, :]
                if n % 8 == 0:
                    dve.wait_ge(sem(f"pad{s}"), i + 1)
                tap = cw[:, j, ds(16 * s + f + 2 * i, 1)]
                src = pad[:, f, j:j + T]
                if j:
                    dve.wait_ge(sem("taps"), 18 * i + 6 * s + 2 * (j - 1) + f + 1)
                name = f"conv{s}" if j == 3 else "taps"
                if j == 0:
                    dve.tensor_scalar(dst, src, tap, None, ALU.mult).then_inc(sem(name), 1)
                else:
                    dve.scalar_tensor_tensor(dst, src, tap, dst, ALU.mult, ALU.add).then_inc(sem(name), 1)

            def qk_front(k, i):
                if k in (27, 28):
                    th, dst, name = ((AT, cq, "silq"), (Am, ck, "silk"))[k - 27]
                    dve.wait_ge(sem("tanh"), nth("tanh", k - 27, i))
                    dve.scalar_tensor_tensor(flat(dst[:]), flat(th[:]), 1.0, flat(dst[:]), ALU.add,
                                             ALU.mult).then_inc(sem(name), 1)
                elif k == 29:
                    dve.tensor_tensor(blocks(Ym[:]),
                                      cst[:, C_CUM:C_CUM + P].unsqueeze(1).unsqueeze(1).to_broadcast([P, 2, TT, P]),
                                      per_row(graw, i), ALU.mult).then_inc(sem("gl"), 1)

            def chain_k(k, p):
                if k == 0:
                    for n, (th, dst, name) in enumerate(((Tm, cv, "silv"), (Um, zb, "silz"))):
                        dve.wait_ge(sem("tanh"), nth("tanh", 2 + n, p))
                        dve.scalar_tensor_tensor(flat(dst[:]), flat(th[:]), 1.0, flat(dst[:]), ALU.add,
                                                 ALU.mult).then_inc(sem(name), 1)
                elif k == "norms":
                    dve.wait_ge(sem("G"), p + 1)
                    dve.tensor_tensor(Am[:], C[:, 2, :].rearrange("p (x c) -> p x c", x=4),
                                      four(cst[:, C_CAUSAL:C_CAUSAL + P]), ALU.add).then_inc(sem("am"), 1)
                    dve.wait_ge(sem("rnk"), p + 1)
                    dve.tensor_tensor(flat(kh[:]), flat(ck[:]), flat(kh[:]), ALU.mult).then_inc(sem("khat"), 1)
                    dve.wait_ge(sem("rnq"), p + 1)
                    dve.tensor_tensor(flat(qh[:]), flat(cq[:]), flat(qh[:]), ALU.mult).then_inc(sem("qhat"), 1)
                elif k == 1:
                    dve.wait_ge(sem("v_rows"), p + 1)
                    dve.tensor_tensor(blocks(bv[:]), blocks(C[:, 3, :]), per_row(bhalf, p),
                                      ALU.mult).then_inc(sem("bv"), 1)
                elif k == 2:
                    dve.wait_ge(sem("egb"), p + 1)
                    dve.wait_ge(sem("qhat"), p + 1)
                    dve.tensor_tensor(flat(qd[:]), flat(qh[:]), flat(egb[:]), ALU.mult).then_inc(sem("qdec"), 1)
                elif k == 3:
                    dve.wait_ge(sem("E"), p + 1)
                    dve.wait_ge(sem("QKp"), p + 1)
                    dve.tensor_tensor(flat(QK[:]), C[:, 1, :], flat(AT[:]), ALU.mult).then_inc(sem("QKm"), 1)
                    dve.wait_ge(sem("KK"), p + 1)
                    for x in range(4):
                        h, t = x // 2, x % 2
                        a = dve.scalar_tensor_tensor(out=Am[:, x, :], in0=C[:, 0, P * x:P * x + P],
                                                     scalar=beta[:, t, ds(2 * p + h, 1)], in1=AT[:, x, :],
                                                     op0=ALU.mult, op1=ALU.mult)
                    a.then_inc(sem("A"), 1)
                    dve.wait_ge(sem("k_rows"), p + 1)
                    dve.tensor_tensor(blocks(kd[:]), blocks(C[:, 3, :]), per_row(kdecs, p),
                                      ALU.mult).then_inc(sem("kdec"), 1)
                    dve.wait_ge(sem("A"), p + 1)
                    dve.tensor_tensor(Tm[:], Am[:], four(negm[0]), ALU.mult).then_inc(sem("t_masked"), 1)
                    dve.wait_ge(sem("t_masked"), p + 1)
                    dve.tensor_tensor(Tm[:], Tm[:], four(ident), ALU.add).then_inc(sem("inverse"), 1)
                elif k == 4:
                    dve.wait_ge(sem("ATc"), p + 1)
                    dve.tensor_tensor(Um[:], AT[:], four(negmt[0]), ALU.mult).then_inc(sem("u_masked"), 1)
                    dve.wait_ge(sem("u_masked"), p + 1)
                    dve.tensor_tensor(Um[:], Um[:], four(ident), ALU.add).then_inc(sem("inverse_t"), 1)
                elif k in (6, 8, 10, 12, 14):
                    n = (k - 4) // 2
                    if n < 5:
                        dve.wait_ge(sem("x_prod"), nth("x_prod", n, p))
                        dve.wait_ge(sem("inverse"), nth("inverse", n - 1, p))
                        dve.tensor_tensor(flat(Tm[:]), C[:, 0, :], flat(Tm[:]), ALU.add).then_inc(sem("inverse"), 1)
                    dve.wait_ge(sem("xt_prod"), nth("xt_prod", n, p))
                    dve.wait_ge(sem("inverse_t"), nth("inverse_t", n - 1, p))
                    dve.tensor_tensor(flat(Um[:]), C[:, 1, :], flat(Um[:]), ALU.add).then_inc(sem("inverse_t"), 1)
                elif k in (17, 20, 23):
                    c = (k - 14) // 3
                    R = slice(CH * (c % 2), CH * (c % 2) + CH)
                    dve.wait_ge(sem("ks_prod"), nth("ks_prod", c, p))
                    for h in range(2):
                        r = dve.scalar_tensor_tensor(out=rr[R, h, :], in0=C[R, 1, h * P:h * P + P],
                                                     scalar=nbeg[R, c // 2, ds(2 * p + h, 1)], in1=bv[R, 2 * h + c // 2, :],
                                                     op0=ALU.mult, op1=ALU.add)
                    r.then_inc(sem("rhs"), 1)
                elif k == 16:
                    dve.wait_ge(sem("o_prod"), nth("o_prod", 0, p))
                    dve.tensor_scalar(flat(S[:]), C[:, 0, 0:256], 1.0, None, ALU.mult).then_inc(sem("state"), 1)
                elif k in (19, 22):
                    c = (k - 16) // 3
                    dve.wait_ge(sem("o_prod"), nth("o_prod", c, p))
                    dve.wait_ge(sem("state"), nth("state", c - 1, p))
                    for h in range(2):
                        r = dve.scalar_tensor_tensor(out=S[:, h, :], in0=S[:, h, :], scalar=dall[:, c, ds(2 * p + h, 1)],
                                                     in1=C[:, 0, h * P:h * P + P], op0=ALU.mult, op1=ALU.add)
                    r.then_inc(sem("state"), 1)
                elif k == 28:
                    dve.wait_ge(sem("rno"), p + 1)
                    dve.tensor_tensor(flat(tmp[:]), C[:, 3, :], flat(tmu[:]), ALU.mult).then_inc(sem("o_scaled"), 1)
                    dve.wait_ge(sem("o_scaled"), p + 1)
                    dve.scalar_tensor_tensor(flat2(odn[:, ds(2 * p, 2), :]), flat(tmp[:]), ghalf[:, 0:1], flat(zb[:]),
                                             ALU.mult, ALU.mult).then_inc(sem("on"), 1)

            def att_k(k, i):
                if k == 3:
                    t = i % TT
                    q = qbuf[:, ds(i, 1), :].rearrange("p o (h c) -> p (o h) c", c=32)
                    tc = flat(sE[:]).rearrange("p (h c) -> p h c", c=32)
                    ts = flat(sO[:]).rearrange("p (h c) -> p h c", c=32)
                    cos = cst[:, ds(C_COS + 32 * t, 32)].unsqueeze(1).to_broadcast([P, 16, 32])
                    sin = cst[:, ds(C_SIN + 32 * t, 32)].unsqueeze(1).to_broadcast([P, 16, 32])
                    dve.tensor_tensor(tc, q, cos, ALU.mult).then_inc(sem("q_cs"), 1)
                    dve.tensor_tensor(ts, q, sin, ALU.mult).then_inc(sem("q_cs"), 1)
                    dve.wait_ge(sem("q_cs"), 2 * i + 2)
                    tc = tc.rearrange("p (h a) c -> p h a c", a=2)
                    ts = ts.rearrange("p (h a) c -> p h a c", a=2)
                    dve.tensor_tensor(qr[:, :, 0:32], tc[:, :, 0], ts[:, :, 1], ALU.subtract)
                    dve.tensor_tensor(qr[:, :, 32:64], tc[:, :, 1], ts[:, :, 0], ALU.add).then_inc(sem("qrot"), 1)
                elif k == 5:
                    dve.tensor_scalar(kS[:], kTall[:, ds(i, 1), :].rearrange("p o n -> p (o n)"), 1.0, None, ALU.mult)
                    dve.tensor_scalar(vS[:], vall[:, ds(i, 1), :, :].rearrange("p o n d -> p (o n) d"), 1.0, None,
                                      ALU.mult).then_inc(sem("kvS"), 1)
                elif k == 7:
                    dve.wait_ge(sem("sc01"), i + 1)
                    s = C[:, 3, :].rearrange("p (r c) -> p r c", r=4)
                    dve.tensor_scalar(sE[:, :, 0:CH], s[:, :, 0:CH], cst[:, ds(C_PREV + i, 1)], None, ALU.add)
                    dve.tensor_scalar(sE[:, :, CH:], s[:, :, CH:], 1.0, None, ALU.mult).then_inc(sem("sE"), 1)
                elif k == 10:
                    dve.wait_ge(sem("sE"), i + 1)
                    dve.tensor_reduce(sm[:, 0, 0:4], sE[:], AX.X, ALU.max).then_inc(sem("row_max"), 1)
                    dve.wait_ge(sem("sO"), i + 1)
                    dve.tensor_reduce(sm[:, 0, 4:8], sO[:], AX.X, ALU.max).then_inc(sem("row_max"), 1)
                    dve.wait_ge(sem("row_max"), 2 * i + 2)
                    sk = sinks[:, ds(i, 1), :].rearrange("p o q -> p (o q)")
                    dve.scalar_tensor_tensor(sm[:, 1, :], sm[:, 0, :], ATT_SCALE, sk, ALU.mult,
                                             ALU.max).then_inc(sem("kept_max"), 1)
                    dve.wait_ge(sem("kept_max"), i + 1)
                    dve.tensor_scalar(sm[:, 2, :], sm[:, 1, :], -1.0, None, ALU.mult)
                    dve.tensor_tensor(sm[:, 3, :], sk, sm[:, 1, :], ALU.subtract).then_inc(sem("nmax"), 1)
                elif k in (12, 13):
                    n = k - 12
                    dve.wait_ge(sem(f"exp{n}"), i + 1)
                    c = slice(4 * n, 4 * n + 4)
                    dve.tensor_tensor(sm[:, 6, c], sm[:, 4, c], sm[:, 5, c], ALU.add).then_inc(sem("row_sum"), 1)
                    dve.wait_ge(sem("row_sum"), 2 * i + n + 1)
                    dve.reciprocal(sm[:, 7, c], sm[:, 6, c]).then_inc(sem("row_inv"), 1)
                    dve.wait_ge(sem("row_inv"), 2 * i + n + 1)
                    m = (sE, sO)[n]
                    dve.tensor_tensor(m[:], m[:], sm[:, 7, c].unsqueeze(2).to_broadcast([P, 4, P]),
                                      ALU.mult).then_inc(sem(f"prob{n}"), 1)

            def mixer_turn(i, chain):
                pos = Pos(4 * U_LOOP + LEAD, 32, i)
                for k in range(32):
                    split(pos, k)
                    if chain:
                        if k == 0:
                            chain_k(0, i - 1)
                        elif k > LAG:
                            chain_k(k - LAG, i - 1)
                        if k == NORMS:
                            chain_k("norms", i - 1)
                    att_k(k - LAG, i)
                    qk_front(k, i)
                    conv(i, k)
                    if k == 31:
                        conv(i, 32)

            dve.wait_ge(sem("kT_out"), 8)
            dve.wait_ge(sem("v_moved"), 48)
            mixer_turn(0, False)
            with dve.Fori(1, PAIRS) as i:
                mixer_turn(i, True)
            for k in range(30):
                chain_k(k, PAIRS - 1)
                if k == 0:
                    chain_k("norms", PAIRS - 1)
                if k in TAIL:
                    split(Pos(4 * U_YA + LEAD), TAIL.index(k))

            for b in range(8):
                dve.wait_ge(sem("b_hi"), b + 1)
                dve.tensor_tensor(bl[:, 2 * b:2 * b + 2, :].rearrange("p u (t c) -> p u t c", t=TT), att_cols(b),
                                  bh[:, 2 * b:2 * b + 2, :].rearrange("p u (t c) -> p u t c", t=TT).bitcast(F32),
                                  ALU.subtract).then_inc(sem("b_lo"), 1)
            def gated_a(j, start=0):
                for k in range(start, 16):
                    split(Pos(4 * U_YA + LEAD, 16, j), k)
                dve.wait_ge(sem("quarter_done"), 4 * U_YA + 16 + 16 * j)
                dve.wait_ge(sem("gate"), j + 1)
                dve.scalar_tensor_tensor(merged[:, ds(2 * j, 2), :], gt[:, 0], 1.0, dense[:, 0:2, 0:T], ALU.add,
                                         ALU.mult).then_inc(sem("prod"), 1)
            gated_a(0, start=8)
            with dve.Fori(1, 8) as j:
                gated_a(j)
            for b in range(8):
                dve.wait_ge(sem("b_hi"), b + 9)
                dve.tensor_tensor(flat(bl[:, 2 * b:2 * b + 2, :]), flat(odn[:, 2 * b:2 * b + 2, :]),
                                  flat(bh[:, 2 * b:2 * b + 2, :]).bitcast(F32), ALU.subtract).then_inc(sem("b_lo"), 1)
            with dve.Fori(0, 8) as j:
                for k in range(16):
                    split(Pos(4 * U_YD + LEAD, 16, j), k)
                dve.wait_ge(sem("quarter_done"), 4 * U_YD + 16 + 16 * j)
                dve.wait_ge(sem("gate"), j + 9)
                dve.scalar_tensor_tensor(yt[:, 0], gt[:, 0], 1.0, dense[:, 0:2, 0:T], ALU.add,
                                         ALU.mult).then_inc(sem("branch_d"), 1)
                dve.wait_ge(sem("branch_d"), j + 1)
                m = merged[:, ds(2 * j, 2), :]
                dve.tensor_tensor(m, m, yt[:, 0], ALU.add).then_inc(sem("prod"), 1)
            for b in range(8):
                dve.wait_ge(sem("m_hi"), b + 1)
                dve.scalar_tensor_tensor(flat(xl[:, 2 * b:2 * b + 2, :]), flat(merged[:, 2 * b:2 * b + 2, :]), 0.5,
                                         flat(xh[:, 2 * b:2 * b + 2, :]).bitcast(F32), ALU.mult,
                                         ALU.subtract).then_inc(sem("m_lo"), 1)

            def norm(parts, name, g, b, stats):
                for t, c in parts:
                    x = res[:, t, c]
                    dve.scalar_tensor_tensor(x, x, stats[:, t, 24:25], g[:, c], ALU.subtract,
                                             ALU.mult).then_inc(sem(own("norm")), 1)
                first = steps["norm"] - len(parts)
                for n, (t, c) in enumerate(parts):
                    dve.wait_ge(sem("norm"), first + n + 1)
                    x = res[:, t, c]
                    dve.scalar_tensor_tensor(x, x, stats[:, t, 27:28], b[:, c], ALU.mult, ALU.add).then_inc(sem(name), 1)

            def inverse_deviation(which, stats):
                for t in range(TT):
                    dve.wait_ge(sem("deviation"), 2 * which + t - 1)
                    dve.reciprocal(stats[:, t, 27:28], stats[:, t, 26:27]).then_inc(sem(own("norm")), 1)

            def statistics(which, t, stats):
                dve.bn_aggr(stats[:, t, 24:26], stats[:, t, 0:24]).then_inc(sem("variance"), 1)

            for c in range(4):
                for k in range(16):
                    split(Pos(4 * U_OUT + LEAD), 16 * c + k)
                dve.wait_ge(sem("quarter_done"), 4 * U_OUT + 16 * (c + 1))
                if c == 0:
                    dve.wait_ge(sem("res_in"), 16)
                b0 = 2 * ((c + 1) % 2)
                x = res[:, :, 512 * c:512 * c + 512]
                dve.scalar_tensor_tensor(x, x, ALPHA, dense[:, b0:b0 + 2, :], ALU.mult,
                                         ALU.add).then_inc(sem("mix_out"), 1)
                dve.wait_ge(sem("mix_out"), c + 1)
                for t in range(TT):
                    dve.bn_stats(lns[:, t, 6 * c:6 * c + 6], res[:, t, 512 * c:512 * c + 512]).then_inc(sem("stats"), 1)
            dve.wait_ge(sem("stats"), 8)
            dve.wait_ge(sem("ln1_in"), 32)
            for t in range(TT):
                statistics(1, t, lns)
            inverse_deviation(1, lns)
            for c in range(4):
                norm([(t, slice(512 * c, 512 * c + 512)) for t in range(TT)], "h1_rows", lng, lnb, lns)
            for b in range(8):
                dve.wait_ge(sem("h1_hi"), b + 1)
                dve.tensor_tensor(flat(xl[:, 2 * b:2 * b + 2, :]), dense[:, b % 4, :],
                                  flat(xh[:, 2 * b:2 * b + 2, :]).bitcast(F32),
                                  ALU.subtract).then_inc(sem("h1_lo"), 1)

            def ple_gate(g):
                dve.wait_ge(sem("quarter_done"), 4 * U_PLE + GATE_AT[g] + 16)
                b0 = 2 * ((g + 1) % 2)
                dve.scalar_tensor_tensor(pg[:, g % 2], dense[:, b0:b0 + 2, :], 1.0,
                                         pb[:, 512 * g:512 * g + 512].unsqueeze(1).to_broadcast([P, TT, 512]),
                                         ALU.mult, ALU.add).then_inc(sem("pgate"), 1)

            def ple_add(g):
                dve.wait_ge(sem("ptanh"), g + 1)
                dve.wait_ge(sem("quarter_done"), 4 * U_PLE + P_AT[g // 2] + 4)
                c = g % 2
                dve.scalar_tensor_tensor(pg[:, c], pg[:, c], 1.0, C[:, 2 * c:2 * c + 2, :], ALU.add,
                                         ALU.mult).then_inc(sem("ple_prod"), 1)
                dve.wait_ge(sem("ple_prod"), g + 1)
                x = res[:, :, 512 * g:512 * g + 512]
                dve.scalar_tensor_tensor(x, x, ALPHA, pg[:, c], ALU.mult, ALU.add).then_inc(sem("ple_out"), 1)

            dve.wait_ge(sem("pb_in"), 16)
            dve.wait_ge(sem("h1_rows"), 8)
            dve.wait_ge(sem("h1_cols"), 8)
            for n in range(72):
                split(Pos(4 * U_PLE + LEAD), n)
                if n in (19, 35, 51):
                    ple_gate((n - 19) // 16)
                elif n in (21, 37, 56):
                    ple_add((n - 20) // 16)
            ple_gate(3)
            ple_add(3)

            def ffn_turn(f):
                dve.wait_ge(sem("quarter_done"), 4 * U_FFN + 16 + 16 * f)
                dve.wait_ge(sem("ff_gate"), f + 1)
                dve.tensor_tensor(ff[:, 1], ff[:, 0], dense[:, 0:2, 0:T], ALU.mult).then_inc(sem("ff_prod"), 1)
                dve.wait_ge(sem("hid_hi"), f + 1)
                dve.tensor_tensor(hl[:, ds(2 * f, 2), :], ff[:, 1], hh[:, ds(2 * f, 2), :].bitcast(F32),
                                  ALU.subtract).then_inc(sem("hid_lo"), 1)
            with dve.Fori(0, FF // 256) as f:
                for k in range(16):
                    split(Pos(4 * U_FFN + LEAD, 16, f), k)
                ffn_turn(f)

            for c in range(4):
                for k in range(FT):
                    if FT * c + k + LEAD < 4 * FT:
                        split(Pos(4 * U_DOWN + LEAD), FT * c + k)
                dve.wait_ge(sem("quarter_done"), 4 * U_DOWN + FT * (c + 1))
                b0 = 2 * ((c + 1) % 2)
                x = res[:, :, 512 * c:512 * c + 512]
                dve.tensor_tensor(x, x, dense[:, b0:b0 + 2, :], ALU.add).then_inc(sem("down_out"), 1)
                dve.wait_ge(sem("down_out"), c + 1)
                for t in range(TT):
                    dve.bn_stats(lnst[:, t, 6 * c:6 * c + 6], res[:, t, 512 * c:512 * c + 512]).then_inc(sem("stats"), 1)
            dve.wait_ge(sem("stats"), 16)
            dve.wait_ge(sem("ln2_in"), 32)
            for t in range(TT):
                statistics(2, t, lnst)
            inverse_deviation(2, lnst)
            for t in range(TT):
                norm([(t, slice(1024 * h, 1024 * h + 1024)) for h in range(2)], "out_rows", lng2, lnb2, lnst)


_INS = ['x', 'p', 'w_in', 'b_in', 'att_sinks', 'dn_conv_w', 'dn_a_log', 'dn_dt_bias', 'dn_norm_g', 'w_br_att',
        'w_br_dn', 'w_out', 'ln_mix_g', 'ln_mix_b', 'w_ffn_gate', 'w_ffn_up', 'w_ffn_down', 'w_ple_gate',
        'b_ple_gate', 'w_ple_proj', 'ln_ffn_g', 'ln_ffn_b']


def kernel(**inputs):
    import concourse.bacc as bacc
    from concourse.bass_utils import run_bass_kernel_spmd

    nc = bacc.Bacc("TRN2", target_bir_lowering=False, num_devices=1)
    arrays = {f"in_{name}_dram": np.ascontiguousarray(inputs[name]) for name in _INS}
    arrays["in_consts_dram"] = constants()
    A = {key[3:-5]: nc.dram_tensor(key, a.shape, mybir.dt.from_np(a.dtype), kind="ExternalInput").ap()
         for key, a in arrays.items()}
    out = nc.dram_tensor("out_0_dram", (1, T, D), F32, kind="ExternalOutput").ap()
    build(nc, A, out)
    r = run_bass_kernel_spmd(nc, [arrays], core_ids=[0])
    return r.results[0]["out_0_dram"]
```
